# Optimizing a Trainium2 kernel written in Bass

```python
import jax, jax.numpy as jnp
from jax import lax
import numpy as np

D_MODEL = 1024
BATCH = 1
SEQ = 1024
DEPTH = 2
DEC_BATCH = 8
DEC_SEQ = 4
PAST_LEN = 2048
PAGE_SIZE = 128

N_MIXERS = 4
GROUP_W = D_MODEL // N_MIXERS
HEAD_DIM = 64
N_HEADS = GROUP_W // HEAD_DIM
CONV_W = 3
DIL_PAIRS = ((128, 1), (512, 4), (2048, 16))
DIL_BLOCK = 128
MAX_WINDOW = 2048
DSA_TOPK = 256
DSA_QBLOCK = 128
IDX_HEADS = 4
IDX_DIM = 32
CHUNK = 128
GMLP_GROUPS = 4
ROPE_THETA = 500000.0
ROPE_FRAC = 4
D_FF = -(-8 * D_MODEL // (3 * 256)) * 256
EPS = 1e-6
SPLIT_SIZES = (GROUP_W,) * 9 + (IDX_HEADS * IDX_DIM, IDX_DIM, IDX_HEADS) + (GROUP_W,) * 2
PROJ_COLS = sum(SPLIT_SIZES)
ATTN_SCALE = HEAD_DIM ** -0.5

kernel_name = "hymba_conv_dilated_dsa_gmlp_step"

def rmsnorm(x, g):
    xf = x.astype(jnp.float32)
    y = xf * lax.rsqrt(jnp.mean(xf * xf, axis=-1, keepdims=True) + EPS)
    return (y * g.astype(jnp.float32)).astype(x.dtype)

def layernorm(x, g, b):
    xf = x.astype(jnp.float32)
    mu = jnp.mean(xf, axis=-1, keepdims=True)
    var = jnp.mean(jnp.square(xf - mu), axis=-1, keepdims=True)
    y = (xf - mu) * lax.rsqrt(var + EPS) * g.astype(jnp.float32) + b.astype(jnp.float32)
    return y.astype(x.dtype)

def rope(x, pos):
    rot = x.shape[-1] // ROPE_FRAC
    half = rot // 2
    inv = jnp.float32(ROPE_THETA) ** (-jnp.arange(half, dtype=jnp.float32) / half)
    ang = pos.astype(jnp.float32)[:, None] * inv[None, :]
    cos = jnp.cos(ang)[:, None, :]
    sin = jnp.sin(ang)[:, None, :]
    xf = x.astype(jnp.float32)
    x1, x2 = xf[..., :half], xf[..., half:rot]
    out = jnp.concatenate([x1 * cos - x2 * sin, x2 * cos + x1 * sin, xf[..., rot:]], axis=-1)
    return out.astype(x.dtype)

def split_proj(h, w_in):
    offs = np.cumsum(SPLIT_SIZES)[:-1].tolist()
    return jnp.split(h @ w_in, offs, axis=-1)

def heads(t):
    return t.reshape(t.shape[:-1] + (N_HEADS, HEAD_DIM))

def take_rows(a, idx):
    return jax.vmap(lambda ab, ib: ab[ib])(a, idx)

def conv3(ext, w):
    T = ext.shape[1] - (CONV_W - 1)
    return sum(w[i] * ext[:, i:i + T] for i in range(CONV_W))

def dilated_prompt(q, k, v, window, dil):
    B, S, H, Dh = q.shape
    span = window // dil
    unit = dil * DIL_BLOCK
    Lp = -(-S // unit) * unit
    nb = Lp // unit

    def classes(t):
        t = jnp.pad(t, ((0, 0), (0, Lp - S), (0, 0), (0, 0)))
        t = t.reshape(B, Lp // dil, dil, H, Dh).transpose(0, 2, 1, 3, 4)
        return t.reshape(B, dil, nb, DIL_BLOCK, H, Dh)

    def with_prev(t):
        prev = jnp.pad(t[:, :, :-1], ((0, 0), (0, 0), (1, 0), (0, 0), (0, 0), (0, 0)))
        return jnp.concatenate([prev, t], axis=3)

    qc = classes(q)
    kk = with_prev(classes(k))
    vv = with_prev(classes(v))
    s = jnp.einsum('brnqhd,brnkhd->brnhqk', qc, kk).astype(jnp.float32) * ATTN_SCALE
    i = jnp.arange(DIL_BLOCK)[:, None]
    j = jnp.arange(2 * DIL_BLOCK)[None, :]
    gap = DIL_BLOCK + i - j
    blk_ok = (jnp.arange(nb)[:, None, None] > 0) | (j[None] >= DIL_BLOCK)
    valid = (gap >= 0) & (gap <= span) & blk_ok
    s = jnp.where(valid[None, None, :, None], s, -jnp.inf)
    lse = jax.nn.logsumexp(s, axis=-1)
    p = jnp.exp(s - lse[..., None])
    o = jnp.einsum('brnhqk,brnkhd->brnqhd', p, vv.astype(jnp.float32))
    o = o.reshape(B, dil, Lp // dil, H, Dh).transpose(0, 2, 1, 3, 4).reshape(B, Lp, H, Dh)[:, :S]
    lse = lse.transpose(0, 1, 2, 4, 3).reshape(B, dil, Lp // dil, H)
    lse = lse.transpose(0, 2, 1, 3).reshape(B, Lp, H)[:, :S]
    return o, lse

def dilated_sample(q, k_ext, v_ext, window, dil):
    T = q.shape[1]
    wb = k_ext.shape[1] - T
    span = window // dil
    idx = wb + jnp.arange(T)[:, None] - dil * jnp.arange(span + 1)[None, :]
    valid = idx >= 0
    idxc = jnp.maximum(idx, 0)
    kg = k_ext[:, idxc]
    vg = v_ext[:, idxc]
    s = jnp.einsum('bthd,btjhd->bthj', q, kg).astype(jnp.float32) * ATTN_SCALE
    s = jnp.where(valid[None, :, None, :], s, -jnp.inf)
    lse = jax.nn.logsumexp(s, axis=-1)
    p = jnp.exp(s - lse[..., None])
    o = jnp.einsum('bthj,btjhd->bthd', p, vg.astype(jnp.float32))
    return o, lse

def merge_by_denominator(outs, lses):
    wts = jax.nn.softmax(jnp.stack(lses), axis=0)
    return jnp.sum(wts[..., None] * jnp.stack(outs), axis=0)

def indexer_scores(qi, wi, ki):
    sc = jax.nn.relu(jnp.einsum('bthd,bsd->bths', qi.astype(jnp.float32), ki.astype(jnp.float32)))
    return jnp.einsum('bth,bths->bts', wi.astype(jnp.float32), sc)

def attend_gathered(q, kg, vg, valid):
    s = jnp.einsum('bthd,btkhd->bthk', q, kg).astype(jnp.float32) * ATTN_SCALE
    s = jnp.where(valid[:, :, None, :], s, -jnp.inf)
    p = jax.nn.softmax(s, axis=-1)
    return jnp.einsum('bthk,btkhd->bthd', p.astype(vg.dtype), vg)

def dsa_prompt(q, k, v, qi, ki, wi):
    B, S = q.shape[:2]
    topk = min(DSA_TOPK, S // 4)
    nb = S // DSA_QBLOCK

    def blockify(t):
        return jnp.moveaxis(t.reshape((B, nb, DSA_QBLOCK) + t.shape[2:]), 1, 0)

    tpos = jnp.arange(S, dtype=jnp.int32).reshape(nb, DSA_QBLOCK)
    spos = jnp.arange(S, dtype=jnp.int32)

    def one_block(args):
        qb, qib, wib, tp = args
        I = indexer_scores(qib, wib, ki)
        I = jnp.where(spos[None, None, :] <= tp[None, :, None], I, -jnp.inf)
        _, idx = lax.top_k(I, topk)
        valid = idx <= tp[None, :, None]
        return attend_gathered(qb, take_rows(k, idx), take_rows(v, idx), valid)

    out = lax.map(one_block, (blockify(q), blockify(qi), blockify(wi), tpos))
    return jnp.moveaxis(out, 0, 1).reshape(B, S, N_HEADS, HEAD_DIM)

def dsa_sample(q, k_new, v_new, qi, ki_new, wi, ck, cv, cki, page_table):
    DB, T = q.shape[:2]
    page = ck.shape[1]
    P = page_table.shape[1] * page
    L = P + T
    topk = min(DSA_TOPK, L // 4)
    ki_past = cki[page_table].reshape(DB, P, IDX_DIM)
    ki_all = jnp.concatenate([ki_past, ki_new.astype(ki_past.dtype)], axis=1)
    tp = P + jnp.arange(T, dtype=jnp.int32)
    I = indexer_scores(qi, wi, ki_all)
    I = jnp.where(jnp.arange(L, dtype=jnp.int32)[None, None, :] <= tp[None, :, None], I, -jnp.inf)
    _, idx = lax.top_k(I, topk)
    valid = idx <= tp[None, :, None]
    in_past = idx < P
    pidx = jnp.minimum(idx, P - 1)
    phys = jnp.take_along_axis(page_table, (pidx // page).reshape(DB, -1), axis=1).reshape(idx.shape)
    off = pidx % page
    nidx = jnp.clip(idx - P, 0, T - 1)
    kg = jnp.where(in_past[..., None, None], ck[phys, off], take_rows(k_new, nidx).astype(ck.dtype))
    vg = jnp.where(in_past[..., None, None], cv[phys, off], take_rows(v_new, nidx).astype(cv.dtype))
    return attend_gathered(q, kg, vg, valid)

def spatial_gate(vn, w_s, b_s):
    B, S = vn.shape[:2]
    T = min(S, CHUNK)
    vc = vn.reshape(B, S // T, T, GMLP_GROUPS, GROUP_W // GMLP_GROUPS)
    wm = (w_s * jnp.tril(jnp.ones((CHUNK, CHUNK), w_s.dtype)))[:, :T, :T]
    s = jnp.einsum('gts,bnsgc->bntgc', wm, vc) + b_s[:, :T].T[None, None, :, :, None]
    return s.reshape(B, S, GROUP_W)

def mixer_prompt(h, w_in, conv_w, ln_g, ln_b, w_s, b_s):
    (a_h, a_b, a_c, b_q, b_k, b_v, c_q, c_k, c_v, c_qi, c_ki, c_wi, d_u, d_v) = split_proj(h, w_in)
    B, S = h.shape[:2]
    pos = jnp.arange(S, dtype=jnp.int32)
    u = a_c * a_h
    ext = jnp.pad(u, ((0, 0), (CONV_W - 1, 0), (0, 0)))
    out_a = a_b * conv3(ext, conv_w)
    st_a = ext[:, -(CONV_W - 1):]
    qb, kb, vb = rope(heads(b_q), pos), rope(heads(b_k), pos), heads(b_v)
    res = [dilated_prompt(qb, kb, vb, w, d) for (w, d) in DIL_PAIRS]
    out_b = merge_by_denominator([r[0] for r in res], [r[1] for r in res]).astype(h.dtype)
    nwin = min(MAX_WINDOW, S)
    qc, kc, vc = rope(heads(c_q), pos), rope(heads(c_k), pos), heads(c_v)
    qi = rope(c_qi.reshape(B, S, IDX_HEADS, IDX_DIM), pos)
    ki = rope(c_ki[:, :, None, :], pos)[:, :, 0]
    out_c = dsa_prompt(qc, kc, vc, qi, ki, c_wi)
    out_d = d_u * spatial_gate(layernorm(d_v, ln_g, ln_b), w_s, b_s)
    m = jnp.concatenate([out_a, out_b.reshape(B, S, GROUP_W), out_c.reshape(B, S, GROUP_W), out_d], axis=-1)
    return m, (st_a, kb[:, S - nwin:], vb[:, S - nwin:], kc, vc, ki)

def mixer_sample(h, conv_buf, kb_buf, vb_buf, ck, cv, cki, page_table, w_in, conv_w, ln_g, ln_b, w_s, b_s):
    (a_h, a_b, a_c, b_q, b_k, b_v, c_q, c_k, c_v, c_qi, c_ki, c_wi, d_u, d_v) = split_proj(h, w_in)
    DB, T = h.shape[:2]
    P = page_table.shape[1] * ck.shape[1]
    pos = P + jnp.arange(T, dtype=jnp.int32)
    u = a_c * a_h
    ext = jnp.concatenate([conv_buf.astype(u.dtype), u], axis=1)
    out_a = a_b * conv3(ext, conv_w)
    st_a = ext[:, -(CONV_W - 1):]
    qb, kb, vb = rope(heads(b_q), pos), rope(heads(b_k), pos), heads(b_v)
    k_ext = jnp.concatenate([kb_buf.astype(kb.dtype), kb], axis=1)
    v_ext = jnp.concatenate([vb_buf.astype(vb.dtype), vb], axis=1)
    res = [dilated_sample(qb, k_ext, v_ext, w, d) for (w, d) in DIL_PAIRS]
    out_b = merge_by_denominator([r[0] for r in res], [r[1] for r in res]).astype(h.dtype)
    qc, kc, vc = rope(heads(c_q), pos), rope(heads(c_k), pos), heads(c_v)
    qi = rope(c_qi.reshape(DB, T, IDX_HEADS, IDX_DIM), pos)
    ki = rope(c_ki[:, :, None, :], pos)[:, :, 0]
    out_c = dsa_sample(qc, kc, vc, qi, ki, c_wi, ck, cv, cki, page_table).astype(h.dtype)
    vn = layernorm(d_v, ln_g, ln_b)
    out_d = d_u * spatial_gate(vn, w_s, b_s)
    m = jnp.concatenate([out_a, out_b.reshape(DB, T, GROUP_W), out_c.reshape(DB, T, GROUP_W), out_d], axis=-1)
    return m, (st_a, kb, vb, kc, vc, ki, vn)

def finish(x, m, w_o, g_post_mix, g_pre_ffn, g_post_ffn, w_gate, w_up, w_down):
    x = x + rmsnorm(m @ w_o, g_post_mix)
    h = rmsnorm(x, g_pre_ffn)
    f = (jax.nn.silu(h @ w_gate) * (h @ w_up)) @ w_down
    return x + rmsnorm(f, g_post_ffn)

def setup_inputs(seed: int = 0) -> dict:
    key = jax.random.key(seed)
    ks = jax.random.split(key, 24)
    n_pages = PAST_LEN // PAGE_SIZE
    n_pool = (5 * DEC_BATCH * n_pages) // 4
    wb = min(MAX_WINDOW, PAST_LEN)

    def nrm(k, shape, s=1.0):
        return s * jax.random.normal(k, shape, jnp.float32)

    perm = jax.random.permutation(ks[8], n_pool)
    page_table = perm[:DEC_BATCH * n_pages].reshape(DEC_BATCH, n_pages).astype(jnp.int32)
    return {
        "x_prompt": nrm(ks[0], (BATCH, SEQ, D_MODEL)),
        "x_sample": nrm(ks[1], (DEC_BATCH, DEC_SEQ, D_MODEL)),
        "cache_conv_a": nrm(ks[2], (DEPTH, DEC_BATCH, CONV_W - 1, GROUP_W)),
        "cache_k_b": nrm(ks[3], (DEPTH, DEC_BATCH, wb, N_HEADS, HEAD_DIM)),
        "cache_v_b": nrm(ks[4], (DEPTH, DEC_BATCH, wb, N_HEADS, HEAD_DIM)),
        "cache_k_c": nrm(ks[5], (DEPTH, n_pool, PAGE_SIZE, N_HEADS, HEAD_DIM)),
        "cache_v_c": nrm(ks[6], (DEPTH, n_pool, PAGE_SIZE, N_HEADS, HEAD_DIM)),
        "cache_kidx_c": nrm(ks[7], (DEPTH, n_pool, PAGE_SIZE, IDX_DIM)),
        "page_table": page_table,
        "w_in": nrm(ks[9], (DEPTH, D_MODEL, PROJ_COLS), D_MODEL ** -0.5),
        "conv_w_a": nrm(ks[10], (DEPTH, CONV_W, GROUP_W), 0.5),
        "ln_g_d": 1.0 + nrm(ks[11], (DEPTH, GROUP_W), 0.05),
        "ln_b_d": nrm(ks[12], (DEPTH, GROUP_W), 0.02),
        "w_s_d": nrm(ks[13], (DEPTH, GMLP_GROUPS, CHUNK, CHUNK), CHUNK ** -0.5),
        "b_s_d": 1.0 + nrm(ks[14], (DEPTH, GMLP_GROUPS, CHUNK), 0.1),
        "w_o": nrm(ks[15], (DEPTH, D_MODEL, D_MODEL), D_MODEL ** -0.5),
        "w_gate": nrm(ks[16], (DEPTH, D_MODEL, D_FF), D_MODEL ** -0.5),
        "w_up": nrm(ks[17], (DEPTH, D_MODEL, D_FF), D_MODEL ** -0.5),
        "w_down": nrm(ks[18], (DEPTH, D_FF, D_MODEL), D_FF ** -0.5),
        "g_pre_mix": 1.0 + nrm(ks[19], (DEPTH, D_MODEL), 0.05),
        "g_post_mix": 1.0 + nrm(ks[20], (DEPTH, D_MODEL), 0.05),
        "g_pre_ffn": 1.0 + nrm(ks[21], (DEPTH, D_MODEL), 0.05),
        "g_post_ffn": 1.0 + nrm(ks[22], (DEPTH, D_MODEL), 0.05),
    }

def reference(x_prompt, x_sample, cache_conv_a, cache_k_b, cache_v_b, cache_k_c, cache_v_c, cache_kidx_c,
              page_table, w_in, conv_w_a, ln_g_d, ln_b_d, w_s_d, b_s_d, w_o, w_gate, w_up, w_down,
              g_pre_mix, g_post_mix, g_pre_ffn, g_post_ffn):
    xp, xs = x_prompt, x_sample
    p_states, s_states = [], []
    for l in range(DEPTH):
        mixw = (w_in[l], conv_w_a[l], ln_g_d[l], ln_b_d[l], w_s_d[l], b_s_d[l])
        ffw = (w_o[l], g_post_mix[l], g_pre_ffn[l], g_post_ffn[l], w_gate[l], w_up[l], w_down[l])
        mp, sp = mixer_prompt(rmsnorm(xp, g_pre_mix[l]), *mixw)
        xp = finish(xp, mp, *ffw)
        ms, ss = mixer_sample(rmsnorm(xs, g_pre_mix[l]), cache_conv_a[l], cache_k_b[l], cache_v_b[l],
                              cache_k_c[l], cache_v_c[l], cache_kidx_c[l], page_table, *mixw)
        xs = finish(xs, ms, *ffw)
        p_states.append(sp)
        s_states.append(ss)
    p_conv_a, p_k_b, p_v_b, p_k_c, p_v_c, p_kidx_c = [jnp.stack(t) for t in zip(*p_states)]
    s_conv_a, s_k_b, s_v_b, s_k_c, s_v_c, s_kidx_c, s_v_d = [jnp.stack(t) for t in zip(*s_states)]
    return (xp, xs, p_conv_a, p_k_b, p_v_b, p_k_c, p_v_c, p_kidx_c,
            s_conv_a, s_k_b, s_v_b, s_k_c, s_v_c, s_kidx_c, s_v_d)


_drawn_inputs = setup_inputs


def setup_inputs(seed=0):
    import zlib

    import numpy as np

    out = dict(_drawn_inputs(seed))
    spreads = {}
    factors = {'ln_b_d': 2.872}
    for name, (base, spread) in spreads.items():
        noise = np.random.default_rng([zlib.crc32(name.encode()), seed]).standard_normal(out[name].shape)
        drawn = base * np.exp(spread * noise) if base else spread * noise
        out[name] = __import__('jax').numpy.asarray(drawn.astype(out[name].dtype))
    for name, factor in factors.items():
        out[name] = (out[name] * factor).astype(out[name].dtype)
    return out
```

```python
from contextlib import ExitStack, contextmanager

import numpy as np
import concourse.bass as bass
from concourse import mybir

ALU = mybir.AluOpType
ACT = mybir.ActivationFunctionType
AX = mybir.AxisListType
F32 = mybir.dt.float32
BF16 = mybir.dt.bfloat16
I32 = mybir.dt.int32

P = 128
D = 1024
DEPTH = 2
SEQ = 1024
DB, DT = 8, 4
PAST = 2048
PAGE = 128
PAGES = PAST // PAGE
POOL_PAGES = 5 * DB * PAGES // 4
GW = 256
NH, HD = 4, 64
IXH, IXD = 4, 32
TOPK = 256
FF = 2816
EPS = 1e-6
SCALE = HD ** -0.5
THETA = 500000.0
NEG = -1e30
TAKEN = -3e38

KC = D // P
FC = FF // P
NS = DB * DT
TILES = SEQ // P + 1
PT = SEQ // P
T = SEQ + NS
TH = T // 3
NBANK = 8

C_AH, C_AB, C_AC, C_BQ, C_BK, C_BV, C_CQ, C_CK, C_CV = (i * GW for i in range(9))
C_IX = 9 * GW
IXW = IXH * IXD + IXD + IXH
C_DU = C_IX + IXW
C_DV = C_DU + GW
PROJ = C_DV + GW

FAR_TILES = (PAST - 512) // 16 * DT // P
NEAR_TILES = 512 // P
BT = FAR_TILES + NEAR_TILES
CT = PAGES


def tok(n):
    return P if n < PT else NS


def cols(n):
    return slice(n * P, n * P + tok(n))


def log_count(gap):
    m = np.zeros(gap.shape, np.float32)
    for window, dil in ((128, 1), (512, 4), (2048, 16)):
        m += (gap >= 0) & (gap <= window) & (gap % dil == 0)
    return np.where(m > 0, np.log(np.maximum(m, 1)), NEG).astype(np.float32)


def constants():
    i = np.arange(P)
    out = {}
    out["ident"] = np.eye(P, dtype=np.float32)
    out["bias_b"] = log_count(SEQ - P + i[:, None] - np.arange(SEQ)[None, :])
    out["causal"] = np.where(i[None, :] <= i[:, None], 0, NEG).astype(np.float32)
    out["tril_t"] = (i[:, None] <= i[None, :]).astype(np.float32)
    r = np.arange(NS)
    b, t = r // DT, r % DT
    hb, ht = np.tile(b, NH), np.tile(t, NH)
    far = np.arange(FAR_TILES * P)
    far = far // DT * 16 + far % DT
    near = PAST - 512 + np.arange(512)
    key = np.concatenate([far, near])
    own = hb[:, None] == b[None, :]
    new = np.where(own, log_count(np.where(own, ht[:, None] - t[None, :], -1)), NEG)
    out["bias_sb"] = np.concatenate([log_count(PAST + ht[:, None] - key[None, :]), new], 1).astype(np.float32)
    see = (b[:, None] == b[None, :]) & (t[None, :] <= t[:, None])
    out["new_ok"] = np.where(see, 0, NEG).astype(np.float32)
    out["own_col"] = np.tile((b[None, :] == np.arange(DB)[:, None]).astype(np.float32)[:, None, :],
                             (1, NH, 1)).reshape(1, DB * P).repeat(P, 0)
    out["rep_heads"] = np.tile(np.eye(NS, dtype=np.float32), (1, NH))
    out["sum_heads"] = out["rep_heads"].T.copy()
    out["rep_step"] = (np.arange(DT)[:, None] == t[None, :]).astype(np.float32)
    out["own_step"] = ((b[:, None] == b[None, :]) & (t[:, None] <= t[None, :])).astype(np.float32)

    pos = np.zeros((TILES, P), np.float32)
    pos[:PT] = np.arange(SEQ).reshape(PT, P)
    pos[PT, :NS] = PAST + t
    for name, half in (("rope_h", HD // 8), ("rope_i", IXD // 8)):
        inv = np.float32(THETA) ** (-np.arange(half, dtype=np.float32) / np.float32(half))
        ang = pos[:, :, None] * inv[None, None, :].astype(np.float32)
        c, s = np.cos(ang), np.sin(ang)
        tab = np.concatenate([c, c, -s, s], -1)
        out[name] = np.ascontiguousarray(tab.transpose(1, 0, 2).reshape(P, -1)).astype(np.float32)
    return out


CONST = constants()


def small(nc, why="small or strided by nature"):
    return nc.allow_non_contiguous_dma(reason=why)


class Shared:
    pass


def program(nc, io):
    nc.disable_value_cache = True
    with ExitStack() as es:
        es.enter_context(small(nc))
        c = Shared()
        c.nc, c.io = nc, io

        def sb(name, shape, dt=F32, stack=es):
            return stack.enter_context(nc.sbuf_tensor(name, shape, dt))

        def sem(name):
            s = es.enter_context(nc.semaphore(name))
            return s

        @contextmanager
        def phase():
            with ExitStack() as st:
                c.phase_sems = []
                c.layer_sem = lambda name: c.phase_sems.append(st.enter_context(nc.semaphore(name))) or c.phase_sems[-1]
                yield st
                for s in c.phase_sems:
                    nc.sync.sem_clear(s)
                nc.all_engine_barrier()

        c.sb = sb
        c.ps = es.enter_context(nc.psum_tensor("ps", [P, NBANK, 512], F32))
        c.xpark = nc.dram_tensor("xpark", (P, KC * T), F32, kind="Internal").ap()
        c.ident = sb("ident", [P, P])
        c.ones = sb("ones", [P, P])
        c.eps = sb("eps", [P, 1])
        c.rope_h = sb("rope_h", [P, TILES, HD // 2])
        c.rope_i = sb("rope_i", [P, TILES, IXD // 2])
        c.tables = sb("tables", [1, DB * PAGES], I32)
        c.xT = sb("xT", [P, KC, T])
        c.hT = sb("hT", [P, KC, T])
        with ExitStack() as st:
            load_x(c, sem, st)
        with nc.Fori(0, DEPTH) as layer:
            c.l = layer
            with phase() as st:
                norm_one(c, st)
            with ExitStack() as st_m:
                c.mT = sb("mT", [P, KC, T], stack=st_m)
                with ExitStack() as st_mix:
                    mixer_buffers(c, st_mix)
                    with phase() as st:
                        projections(c, st)
                    with phase() as st:
                        conv_and_gate(c, st)
                    with phase() as st:
                        index_prompt(c, st)
                    with phase() as st:
                        attend_prompt(c, st)
                    with phase() as st:
                        attend_sample(c, st)
                with phase() as st:
                    out_stage(c, st, "wo", io["w_o"], c.mT, KC, "g_post_mix", "g_pre_ffn", c.xpark)
            with ExitStack() as st:
                aT = c.sb("aT", [P, FC, T], stack=st)
                with phase() as st2:
                    ffn_in(c, st2, aT)
                with phase() as st2:
                    out_stage(c, st2, "wd", io["w_down"], aT, FC, "g_post_ffn", None, None)
        with ExitStack() as st:
            store_y(c, sem, st)


def load_x(c, sem, st):
    nc, io = c.nc, c.io
    xt = c.sb("x_tok", [P, 2, D], stack=st)
    xT = c.xT
    const_in, ones_set = sem("const_in"), sem("ones_set")
    x_in = [sem(f"x_in{i}") for i in range(2)]
    turned, copied, parked = sem("x_turned"), sem("x_copied"), sem("x_parked")
    ps = c.ps
    with nc.Block() as block:
        @block.sync
        def _(sp):
            sp.dma_start(c.ident[:, :], io["ident"]).then_inc(const_in, 16)
            sp.dma_start(c.rope_h[:, :, :], io["rope_h"].rearrange("p (n w) -> p n w", n=TILES)).then_inc(const_in, 16)
            sp.dma_start(c.rope_i[:, :, :], io["rope_i"].rearrange("p (n w) -> p n w", n=TILES)).then_inc(const_in, 16)
            sp.dma_start(c.tables[:, :], io["page_table"].rearrange("b p -> (b p)").rearrange("(o n) -> o n", o=1)).then_inc(const_in, 16)
            for n in range(TILES):
                m = tok(n)
                if n >= 2:
                    sp.wait_ge(turned, 2 * (n - 1))
                src = io["x_prompt"][0, n * P:n * P + m, :] if n < PT else io["x_sample"].rearrange("b t d -> (b t) d")
                sp.dma_start(xt[:m, n % 2, :], src).then_inc(x_in[n % 2], 16)
            sp.wait_ge(copied, 2 * TILES)
            sp.dma_start(c.xpark, xT[:, :, :].rearrange("p k t -> p (k t)")).then_inc(parked, 16)
            sp.wait_ge(parked, 16)

        @block.gpsimd
        def _(pool):
            pool.memset(c.ones[:, :], 1.0).then_inc(ones_set, 1)
            pool.memset(c.eps[:, :], EPS).then_inc(ones_set, 1)

        @block.tensor
        def _(pe):
            pe.wait_ge(const_in, 64)
            for n in range(TILES):
                m = tok(n)
                pe.wait_ge(x_in[n % 2], 16 * (n // 2 + 1))
                for half in range(2):
                    i = 2 * n + half
                    if i >= 4:
                        pe.wait_ge(copied, i - 3)
                    for q in range(4):
                        k = 4 * half + q
                        ins = pe.transpose(ps[:, i % 4, q * P:q * P + m], xt[:m, n % 2, k * P:(k + 1) * P], c.ident[:m, :m])
                    ins.then_inc(turned, 1)

        @block.vector
        def _(dve):
            for n in range(TILES):
                for half in range(2):
                    i = 2 * n + half
                    dve.wait_ge(turned, i + 1)
                    dve.tensor_copy(xT[:, 4 * half:4 * half + 4, cols(n)],
                                    ps[:, i % 4, :].rearrange("p (k t) -> p k t", k=4)[:, :, 0:tok(n)]).then_inc(copied, 1)


def store_y(c, sem, st):
    nc, io = c.nc, c.io
    xT = c.xT
    yt = c.sb("y_tok", [P, 2, D], stack=st)
    back = sem("x_back")
    turned, copied = sem("y_turned"), sem("y_copied")
    y_out = [sem(f"y_out{i}") for i in range(2)]
    ps = c.ps
    with nc.Block() as block:
        @block.sync
        def _(sp):
            sp.dma_start(xT[:, :, :].rearrange("p k t -> p (k t)"), c.xpark).then_inc(back, 16)
            for n in range(TILES):
                m = tok(n)
                sp.wait_ge(copied, 2 * (n + 1))
                dst = io["y_prompt"][0, n * P:n * P + m, :] if n < PT else io["y_sample"].rearrange("b t d -> (b t) d")
                sp.dma_start(dst, yt[:m, n % 2, :]).then_inc(y_out[n % 2], 16)
            sp.wait_ge(y_out[0], 16 * ((TILES + 1) // 2))
            sp.wait_ge(y_out[1], 16 * (TILES // 2))

        @block.tensor
        def _(pe):
            pe.wait_ge(back, 16)
            for n in range(TILES):
                m = tok(n)
                for half in range(2):
                    i = 2 * n + half
                    if i >= 4:
                        pe.wait_ge(copied, i - 3)
                    for q in range(4):
                        k = 4 * half + q
                        ins = pe.transpose(ps[:m, i % 4, q * P:(q + 1) * P], xT[:, k, cols(n)], c.ident[:, :])
                    ins.then_inc(turned, 1)

        @block.vector
        def _(dve):
            for n in range(TILES):
                m = tok(n)
                if n >= 2:
                    dve.wait_ge(y_out[n % 2], 16 * (n // 2))
                for half in range(2):
                    i = 2 * n + half
                    dve.wait_ge(turned, i + 1)
                    dve.tensor_copy(yt[:m, n % 2, 512 * half:512 * half + 512], ps[:m, i % 4, :]).then_inc(copied, 1)


def stats_act_square(c, act, sq, src_k, k, ready, used):
    if k >= 2:
        act.wait_ge(used, k - 1)
    act.activation(sq[:, k % 2, :], src_k, ACT.Square).then_inc(ready, 1)


def stats_pe_sum(c, pe, sq, k, bank0, ready, used):
    pe.wait_ge(ready, k + 1)
    for th in range(3):
        ins = pe.matmul(c.ps[:, bank0 + th, 0:TH], c.ones[:, :], sq[:, k % 2, th * TH:(th + 1) * TH],
                        start=(k == 0), stop=(k == KC - 1))
    ins.then_inc(used, 1)


def stats_act_root(c, act, rstd, bank0, used, rooted):
    act.wait_ge(used, KC)
    for th in range(3):
        act.activation(rstd[:, th * TH:(th + 1) * TH], c.ps[:, bank0 + th, 0:TH], ACT.Sqrt,
                       bias=c.eps[:, 0:1], scale=1.0 / D).then_inc(rooted, 1)


def gain(io_g, l):
    return io_g[l].rearrange("(k p) -> p k", p=P)


def norm_one(c, st):
    nc, io, ps = c.nc, c.io, c.ps
    xT = c.xT
    g = c.sb("g_a", [P, KC], stack=st)
    sq = c.sb("sq_a", [P, 2, T], stack=st)
    rstd = c.sb("rstd_a", [P, T], stack=st)
    s = c.layer_sem
    x_in, squared, summed, rooted, inverted, h_done = (s(f"a_{n}") for n in ("x_in", "squared", "summed", "rooted", "inverted", "h_done"))
    with nc.Block() as block:
        @block.sync
        def _(sp):
            sp.dma_start(xT[:, :, :].rearrange("p k t -> p (k t)"), c.xpark).then_inc(x_in, 16)
            sp.dma_start(g[:, :], gain(io["g_pre_mix"], c.l)).then_inc(x_in, 16)

        @block.scalar
        def _(act):
            act.wait_ge(x_in, 32)
            for k in range(KC):
                stats_act_square(c, act, sq, xT[:, k, :], k, squared, summed)
            stats_act_root(c, act, rstd, 0, summed, rooted)

        @block.tensor
        def _(pe):
            for k in range(KC):
                stats_pe_sum(c, pe, sq, k, 0, squared, summed)

        @block.vector
        def _(dve):
            dve.wait_ge(rooted, 3)
            dve.reciprocal(rstd[:, :], rstd[:, :]).then_inc(inverted, 1)
            dve.wait_ge(inverted, 1)
            for k in range(KC):
                dve.scalar_tensor_tensor(out=c.hT[:, k, :], in0=xT[:, k, :], scalar=g[:, k:k + 1], in1=rstd[:, :],
                                         op0=ALU.mult, op1=ALU.mult).then_inc(h_done, 1)


def mixer_buffers(c, st):
    def sb(name, shape, dt=F32):
        return c.sb(name, shape, dt, stack=st)
    c.kT = {"b": c.xT[:, 0:2, :], "c": c.xT[:, 2:4, :]}
    c.qiT = c.xT[:, 4, :]
    c.kiT = c.xT[:, 5, :]
    c.acT = c.xT[:, 6:8, :]
    c.qi_tok = sb("qi_tok", [NS, IXH * IXD])
    c.v = {"b": sb("v_b", [P, TILES, GW]), "c": sb("v_c", [P, TILES, GW])}
    c.chunk = {"b": 2, "c": 4}
    c.wi = sb("wi", [P, TILES, IXH])
    c.mask_c = sb("mask_c", [P, P * PT * (PT + 1) // 2], BF16)
    c.vn = sb("vn", [P, TILES, GW])
    c.ext_p = sb("ext_p", [P, 2, SEQ + 2])
    c.ext_s = sb("ext_s", [P, 2, DB, DT + 2])


def mask_at(n):
    return slice(P * n * (n + 1) // 2, P * (n + 1) * (n + 2) // 2)


def projections(c, st):
    nc, io, ps, hT, l = c.nc, c.io, c.ps, c.hT, c.l
    sb = lambda name, shape: c.sb(name, shape, stack=st)
    W = sb("w_in_slots", [P, 2, KC, 512])
    stage = sb("stage", [P, 2, 512])
    ki4 = sb("ki4", [P, 2, 4, IXD])
    r1, r2 = sb("rope_1", [P, 8, HD // 4]), sb("rope_2", [P, 8, HD // 4])
    st6, mv, ln_r = sb("ln_stats", [P, TILES, 6]), sb("ln_mv", [P, TILES, 2]), sb("ln_r", [P, TILES])
    ln_g, ln_b = sb("ln_g", [P, GW]), sb("ln_b", [P, GW])
    s = c.layer_sem
    w_in = [s(f"w_in{i}") for i in range(2)]
    ln_in = s("ln_in")
    proj_done, proj_freed = s("proj_done"), s("proj_freed")
    rope_1, rope_2, roped = s("rope_1"), s("rope_2"), s("roped")
    tp_done, tp_freed = s("tp_done"), s("tp_freed")
    staged_out = [s(f"staged_out{i}") for i in range(2)]
    v_out = s("v_out")
    mv_set, mv_done, ln_rooted, ln_inv, ln_1, ln_2, ln_done = (s(f"ln_{n}") for n in ("set", "mv", "rooted", "inv", "1", "2", "done"))
    stats_done = s("ln_stats_done")

    groups = [[(C_CV, GW + IXW)], [(C_CQ, 2 * GW)], [(C_BQ, 2 * GW)], [(C_BV, GW), (C_DV, GW)],
              [(C_AH, 2 * GW)], [(C_AC, GW), (C_DU, GW)]]
    TG = 4
    width = [sum(w for _, w in g) for g in groups]
    loads, at = [], [0, 0]
    for g, parts in enumerate(groups):
        at[g % 2] += 16 * len(parts)
        loads.append(at[g % 2])
    items = [(g, n) for g in range(TG) for n in range(TILES)]
    NI = len(items)
    NTP = 3 * TILES
    w_all = io["w_in"][l].rearrange("(k p) n -> p k n", p=P)
    rows = lambda ap, n: ap[0, n * P:(n + 1) * P] if n < PT else None

    def group_load(sp, g):
        o = 0
        for a, w in groups[g]:
            sp.dma_start(W[:, g % 2, :, o:o + w], w_all[:, :, a:a + w]).then_inc(w_in[g % 2], 16)
            o += w

    def kv_rows(name, n):
        if n < PT:
            return io["p_" + name][l][0].rearrange("s h d -> s (h d)")[n * P:(n + 1) * P]
        return io["s_" + name][l].rearrange("b t h d -> (b t) (h d)")

    def kidx_rows(n):
        return io["p_kidx_c"][l][0][n * P:(n + 1) * P] if n < PT else io["s_kidx_c"][l].rearrange("b t d -> (b t) d")

    with nc.Block() as block:
        @block.sync
        def _(sp):
            group_load(sp, 0)
            group_load(sp, 1)
            sp.dma_start(ln_g[:, :], io["ln_g_d"][l].rearrange("(o n) -> o n", o=1).to_broadcast([P, GW])).then_inc(ln_in, 16)
            sp.dma_start(ln_b[:, :], io["ln_b_d"][l].rearrange("(o n) -> o n", o=1).to_broadcast([P, GW])).then_inc(ln_in, 16)
            nv = 0
            for i, (g, n) in enumerate(items):
                m = tok(n)
                if g in (0, 3):
                    sp.wait_ge(proj_freed, i + 1)
                    sp.dma_start(kv_rows("v_c" if g == 0 else "v_b", n), c.v["c" if g == 0 else "b"][:m, n, :]).then_inc(v_out, 16)
                    nv += 1
                if g < 3:
                    sp.wait_ge(roped, i + 1)
                    if g == 0:
                        sp.dma_start(kidx_rows(n), stage[:m, i % 2, 4 * IXD:5 * IXD]).then_inc(staged_out[i % 2], 16)
                    else:
                        sp.dma_start(kv_rows("k_c" if g == 1 else "k_b", n), stage[:m, i % 2, GW:2 * GW]).then_inc(staged_out[i % 2], 16)
                if n == TILES - 1 and g + 2 < len(groups):
                    sp.wait_ge(proj_done, TILES * (g + 1))
                    group_load(sp, g + 2)
            sp.wait_ge(ln_done, TILES)
            sp.dma_start(io["s_v_d"][l].rearrange("b t n -> (b t) n"), c.vn[:NS, PT, :]).then_inc(v_out, 16)
            sp.wait_ge(v_out, 16 * (nv + 1))
            sp.wait_ge(staged_out[0], 16 * ((NTP + 1) // 2))
            sp.wait_ge(staged_out[1], 16 * (NTP // 2))

        @block.tensor
        def _(pe):
            def turn(t):
                g, n = items[t]
                m = tok(n)
                pe.wait_ge(roped, t + 1)
                if t >= 2:
                    pe.wait_ge(tp_freed, t - 1)
                if g == 0:
                    srcs = [stage[:m, t % 2, 0:P], ki4[:m, t % 2, :, :].rearrange("p r d -> p (r d)")]
                else:
                    srcs = [stage[:m, t % 2, q * P:(q + 1) * P] for q in range(4)]
                for q, src in enumerate(srcs):
                    ins = pe.transpose(ps[:, 6 + t % 2, q * P:q * P + m], src, c.ident[:m, :m])
                ins.then_inc(tp_done, 1)

            for i, (g, n) in enumerate(items):
                m = tok(n)
                if n == 0:
                    pe.wait_ge(w_in[g % 2], loads[g])
                if i >= 6:
                    pe.wait_ge(proj_freed, i - 5)
                for k in range(KC):
                    ins = pe.matmul(ps[:m, i % 6, 0:width[g]], hT[:, k, cols(n)], W[:, g % 2, k, 0:width[g]],
                                    start=(k == 0), stop=(k == KC - 1))
                ins.then_inc(proj_done, 1)
                if 1 <= i <= NTP:
                    turn(i - 1)
            for q in range(8):
                g = TG + q // 4
                if q % 4 == 0:
                    pe.wait_ge(w_in[g % 2], loads[g])
                i = NI + 3 * q
                pe.wait_ge(proj_freed, i - 3)
                for k in range(KC):
                    for th in range(3):
                        ins = pe.matmul(ps[:, (i + th) % 6, 0:TH], W[:, g % 2, k, (q % 4) * P:(q % 4 + 1) * P],
                                        hT[:, k, th * TH:(th + 1) * TH], start=(k == 0), stop=(k == KC - 1))
                ins.then_inc(proj_done, 1)

        @block.scalar
        def _(act):
            for i, (g, n) in enumerate(items):
                m = tok(n)
                act.wait_ge(proj_done, i + 1)
                bank = ps[:m, i % 6, :]
                if g in (0, 1, 2) and i >= 2:
                    act.wait_ge(tp_done, i - 1)
                    act.wait_ge(staged_out[i % 2], 16 * ((i - 2) // 2 + 1))
                if g == 0:
                    act.activation(c.v["c"][:m, n, :], bank[:, 0:GW], ACT.Copy)
                    act.activation(stage[:m, i % 2, 0:IXW], bank[:, GW:GW + IXW], ACT.Copy).then_inc(proj_freed, 1)
                elif g < 3:
                    act.activation(stage[:m, i % 2, :], bank[:, 0:2 * GW], ACT.Copy).then_inc(proj_freed, 1)
                else:
                    act.activation(c.v["b"][:m, n, :], bank[:, 0:GW], ACT.Copy)
                    act.activation(c.vn[:m, n, :], bank[:, GW:2 * GW], ACT.Copy).then_inc(proj_freed, 1)
            for q in range(8):
                act.wait_ge(proj_done, NI + q + 1)
                i = NI + 3 * q
                for th in range(3):
                    a, b = th * TH, (th + 1) * TH
                    src = ps[:, (i + th) % 6, :]
                    if q < 2:
                        e = min(b, SEQ)
                        last = act.activation(c.ext_p[:, q, 2 + a:2 + e], src[:, 0:e - a], ACT.Copy)
                        if b > SEQ:
                            last = act.activation(c.ext_s[:, q, :, 2:2 + DT],
                                                  src[:, SEQ - a:TH].rearrange("p (b t) -> p b t", b=DB), ACT.Copy)
                    else:
                        dst = [None, None, c.mT[:, 0], c.mT[:, 1], c.acT[:, 0], c.acT[:, 1], c.mT[:, 6], c.mT[:, 7]][q]
                        last = act.activation(dst[:, a:b], src[:, 0:TH], ACT.Copy)
                    last.then_inc(proj_freed, 1)
            act.wait_ge(mv_done, TILES)
            act.activation(ln_r[:, :], mv[:, :, 1], ACT.Sqrt, bias=c.eps[:, 0:1]).then_inc(ln_rooted, 1)

        @block.vector
        def _(dve):
            def rotate(i):
                g, n = items[i]
                m = tok(n)
                H, w, tab = (5, IXD, c.rope_i) if g == 0 else (8, HD, c.rope_h)
                rot = w // 4
                half = rot // 2
                x = stage[:m, i % 2, 0:H * w].rearrange("p (h w) -> p h w", h=H)
                cs = tab[:m, n, 0:rot].unsqueeze(1).to_broadcast([m, H, rot])
                sn1 = tab[:m, n, rot:rot + half].unsqueeze(1).to_broadcast([m, H, half])
                sn2 = tab[:m, n, rot + half:2 * rot].unsqueeze(1).to_broadcast([m, H, half])
                dve.wait_ge(proj_freed, i + 1)
                if i:
                    dve.wait_ge(roped, i)
                dve.tensor_tensor(r1[:m, 0:H, 0:rot], x[:, :, 0:rot], cs, ALU.mult)
                dve.tensor_tensor(r2[:m, 0:H, 0:half], x[:, :, half:rot], sn1, ALU.mult)
                dve.tensor_tensor(r2[:m, 0:H, half:rot], x[:, :, 0:half], sn2, ALU.mult).then_inc(rope_1, 1)
                dve.wait_ge(rope_1, i + 1)
                last = dve.tensor_tensor(x[:, :, 0:rot], r1[:m, 0:H, 0:rot], r2[:m, 0:H, 0:rot], ALU.add)
                if g == 0:
                    last.then_inc(rope_2, 1)
                    dve.wait_ge(rope_2, i + 1)
                    dve.tensor_copy(ki4[:m, i % 2, :, :], stage[:m, i % 2, 4 * IXD:5 * IXD].unsqueeze(1).to_broadcast([m, 4, IXD]))
                    if n == PT:
                        dve.tensor_copy(c.qi_tok[:, :], stage[:m, i % 2, 0:IXH * IXD])
                    last = dve.tensor_copy(c.wi[:m, n, :], stage[:m, i % 2, 5 * IXD:IXW])
                last.then_inc(roped, 1)

            def unload(t):
                g, n = items[t]
                m = tok(n)
                dve.wait_ge(tp_done, t + 1)
                bank = ps[:, 6 + t % 2, :].rearrange("p (q t) -> p q t", q=4)
                if g == 0:
                    dve.tensor_copy(c.qiT[:, cols(n)], bank[:, 0, 0:m])
                    dve.tensor_copy(c.kiT[:, cols(n)], bank[:, 1, 0:m]).then_inc(tp_freed, 1)
                else:
                    x = "c" if g == 1 else "b"
                    dve.tensor_copy(c.mT[:, c.chunk[x]:c.chunk[x] + 2, cols(n)], bank[:, 0:2, 0:m])
                    dve.tensor_copy(c.kT[x][:, :, cols(n)], bank[:, 2:4, 0:m]).then_inc(tp_freed, 1)

            dve.memset(mv[:, :, :], 1.0).then_inc(mv_set, 1)
            for i in range(NTP):
                rotate(i)
                if i >= 1:
                    unload(i - 1)
            unload(NTP - 1)
            dve.wait_ge(mv_set, 1)
            for n in range(TILES):
                m = tok(n)
                dve.wait_ge(proj_freed, NTP + n + 1)
                dve.bn_stats(st6[:m, n, :], c.vn[:m, n, :]).then_inc(stats_done, 1)
                dve.wait_ge(stats_done, n + 1)
                dve.bn_aggr(mv[:m, n, :], st6[:m, n, :]).then_inc(mv_done, 1)
            dve.wait_ge(ln_rooted, 1)
            dve.reciprocal(ln_r[:, :], ln_r[:, :]).then_inc(ln_inv, 1)
            dve.wait_ge(ln_inv, 1)
            dve.wait_ge(ln_in, 32)
            for n in range(TILES):
                m = tok(n)
                dve.tensor_scalar(c.vn[:m, n, :], c.vn[:m, n, :], mv[:m, n, 0:1], ln_r[:m, n:n + 1],
                                  ALU.subtract, ALU.mult).then_inc(ln_1, 1)
            for n in range(TILES):
                m = tok(n)
                dve.wait_ge(ln_1, n + 1)
                dve.tensor_tensor(c.vn[:m, n, :], c.vn[:m, n, :], ln_g[:m, :], ALU.mult).then_inc(ln_2, 1)
            for n in range(TILES):
                m = tok(n)
                dve.wait_ge(ln_2, n + 1)
                dve.tensor_tensor(c.vn[:m, n, :], c.vn[:m, n, :], ln_b[:m, :], ALU.add).then_inc(ln_done, 1)


def conv_and_gate(c, st):
    nc, io, ps, l = c.nc, c.io, c.ps, c.l
    sb = lambda name, shape: c.sb(name, shape, stack=st)
    cw = sb("conv_w", [P, 2, 3])
    buf = sb("conv_buf", [2 * DB, GW])
    acc_p, acc_s = sb("conv_acc_p", [P, 2, SEQ]), sb("conv_acc_s", [P, 2, DB, DT])
    NST = 2 + 2 * DB
    state, state_t = sb("conv_state", [P, 2, NST]), sb("conv_state_t", [NST, GW])
    ws, wT = sb("w_s", [P, 4, P]), sb("w_sT", [P, 4, P])
    w4 = sb("w_s4", [NS, 4, NS])
    bs = sb("b_s", [P, 2, P])
    gate_p = sb("gate_p", [P, 2, 2, P])
    tril, rep_step, own_step = sb("tril_t", [P, P]), sb("rep_step", [DT, NS]), sb("own_step", [NS, NS])
    s = c.layer_sem
    a_in, d_in = s("conv_in"), s("gate_in")
    buf_turned, buf_set, pad_set, u_done, u2_done = s("buf_turned"), s("buf_set"), s("pad_set"), s("u_done"), s("u2_done")
    tap = s("conv_tap")
    a_done, state_set, state_turned, state_copied, state_out = (s(f"conv_{n}") for n in ("a_done", "state_set", "state_turned", "state_copied", "state_out"))
    ws_turned, ws_masked, w4_made, w4_masked, gated, gate_add, gate_done = (s(f"gate_{n}") for n in ("ws_turned", "ws_masked", "w4_made", "w4_masked", "prod", "add", "done"))

    with nc.Block() as block:
        @block.sync
        def _(sp):
            for k in range(2):
                sp.dma_start(cw[:, k, :], io["conv_w_a"][l].rearrange("i (k p) -> p k i", p=P)[:, k, :]).then_inc(a_in, 16)
            sp.dma_start(buf[:, :], io["cache_conv_a"][l].rearrange("b i n -> (b i) n")).then_inc(a_in, 16)
            sp.dma_start(ws[:, :, :], io["w_s_d"][l].rearrange("g t s -> t g s")).then_inc(d_in, 16)
            sp.dma_start(tril[:, :], io["tril_t"]).then_inc(d_in, 16)
            sp.dma_start(rep_step[:, :], io["rep_step"]).then_inc(d_in, 16)
            sp.dma_start(own_step[:, :], io["own_step"]).then_inc(d_in, 16)
            for g in range(4):
                sp.dma_start(bs[64 * (g % 2):64 * (g % 2) + 64, g // 2, :],
                             io["b_s_d"][l][g:g + 1, :].to_broadcast([64, P])).then_inc(d_in, 16)
            sp.wait_ge(state_copied, 1)
            sp.dma_start(io["p_conv_a"][l].rearrange("b i n -> (b i) n"), state_t[0:2, :]).then_inc(state_out, 16)
            sp.dma_start(io["s_conv_a"][l].rearrange("b i n -> (b i) n"), state_t[2:NST, :]).then_inc(state_out, 16)
            sp.wait_ge(state_out, 32)

        @block.tensor
        def _(pe):
            pe.wait_ge(a_in, 48)
            for k in range(2):
                ins = pe.transpose(ps[:, 0, k * 16:k * 16 + 16], buf[:, k * P:(k + 1) * P], c.ident[:16, :16])
            ins.then_inc(buf_turned, 1)
            pe.wait_ge(d_in, 128)
            for g in range(4):
                ins = pe.transpose(ps[:, 1, g * P:(g + 1) * P], ws[:, g, :], c.ident[:, :])
            ins.then_inc(ws_turned, 1)
            pe.wait_ge(ws_masked, 1)
            pe.matmul(ps[:NS, 2, 0:4 * DT], rep_step[:, :], wT[0:DT, :, 0:DT], start=True, stop=True).then_inc(w4_made, 1)
            for n in range(TILES):
                m = tok(n)
                if n == PT:
                    pe.wait_ge(w4_masked, 4)
                if n >= 2:
                    pe.wait_ge(gate_add, n - 1)
                for g in range(4):
                    rhs = wT[:, g, :] if n < PT else w4[:, g, :]
                    ins = pe.matmul(ps[64 * (g % 2):64 * (g % 2) + 64, 4 + n % 2, (g // 2) * P:(g // 2) * P + m],
                                    c.vn[:m, n, g * 64:(g + 1) * 64], rhs, start=True, stop=True)
                ins.then_inc(gated, 1)
            pe.wait_ge(state_set, 3)
            for k in range(2):
                ins = pe.transpose(ps[:NST, 3, k * P:(k + 1) * P], state[:, k, :], c.ident[:, :])
            ins.then_inc(state_turned, 1)

        @block.vector
        def _(dve):
            dve.memset(c.ext_p[:, :, 0:2], 0.0).then_inc(pad_set, 1)
            dve.wait_ge(buf_turned, 1)
            dve.tensor_copy(c.ext_s[:, :, :, 0:2], ps[:, 0, 0:32].rearrange("p (k b i) -> p k b i", k=2, b=DB)).then_inc(buf_set, 1)
            dve.tensor_tensor(c.ext_p[:, :, 2:], c.ext_p[:, :, 2:], c.acT[:, :, 0:SEQ], ALU.mult).then_inc(u_done, 1)
            for k in range(2):
                dve.tensor_tensor(c.ext_s[:, k, :, 2:], c.ext_s[:, k, :, 2:],
                                  c.acT[:, k, SEQ:].rearrange("p (b t) -> p b t", b=DB), ALU.mult).then_inc(u_done, 1)
            dve.wait_ge(u_done, 3)
            dve.wait_ge(pad_set, 1)
            dve.wait_ge(buf_set, 1)
            dve.tensor_copy(state[:, :, 0:2], c.ext_p[:, :, SEQ:SEQ + 2]).then_inc(state_set, 1)
            for k in range(2):
                dve.tensor_copy(state[:, k, 2:].rearrange("p (b i) -> p b i", b=DB), c.ext_s[:, k, :, DT:DT + 2]).then_inc(state_set, 1)
            nt = 0
            for i in range(3):
                for k in range(2):
                    if i:
                        dve.wait_ge(tap, nt - 3)
                    if i == 0:
                        dve.tensor_scalar(acc_p[:, k, :], c.ext_p[:, k, 0:SEQ], cw[:, k, 0:1], None, ALU.mult).then_inc(tap, 1)
                        dve.tensor_scalar(acc_s[:, k], c.ext_s[:, k, :, 0:DT], cw[:, k, 0:1], None, ALU.mult).then_inc(tap, 1)
                    else:
                        if i:
                            dve.wait_ge(tap, nt - 2)
                        dve.scalar_tensor_tensor(out=acc_p[:, k, :], in0=c.ext_p[:, k, i:i + SEQ], scalar=cw[:, k, i:i + 1],
                                                 in1=acc_p[:, k, :], op0=ALU.mult, op1=ALU.add).then_inc(tap, 1)
                        dve.scalar_tensor_tensor(out=acc_s[:, k], in0=c.ext_s[:, k, :, i:i + DT], scalar=cw[:, k, i:i + 1],
                                                 in1=acc_s[:, k], op0=ALU.mult, op1=ALU.add).then_inc(tap, 1)
                    nt += 2
            dve.wait_ge(tap, 12)
            dve.tensor_tensor(c.mT[:, 0:2, 0:SEQ], c.mT[:, 0:2, 0:SEQ], acc_p[:, :, :], ALU.mult).then_inc(a_done, 1)
            dve.tensor_tensor(c.mT[:, 0:2, SEQ:], c.mT[:, 0:2, SEQ:], acc_s[:, :, :, :].rearrange("p k b t -> p k (b t)"), ALU.mult).then_inc(a_done, 1)
            dve.wait_ge(d_in, 128)
            dve.wait_ge(ws_turned, 1)
            dve.tensor_tensor(wT[:, :, :], ps[:, 1, :].rearrange("p (g t) -> p g t", g=4),
                              tril[:, :].unsqueeze(1).to_broadcast([P, 4, P]), ALU.mult).then_inc(ws_masked, 1)
            dve.wait_ge(w4_made, 1)
            for g in range(4):
                dve.tensor_tensor(w4[:, g, :].rearrange("p (b t) -> p b t", b=DB),
                                  ps[:NS, 2, g * DT:(g + 1) * DT].unsqueeze(1).to_broadcast([NS, DB, DT]),
                                  own_step[:, :].rearrange("p (b t) -> p b t", b=DB), ALU.mult).then_inc(w4_masked, 1)
            for n in range(TILES):
                m = tok(n)
                dve.wait_ge(gated, n + 1)
                for k in range(2):
                    src, dst = ps[:, 4 + n % 2, k * P:k * P + m], gate_p[:, n % 2, k, 0:m]
                    b = bs[:, k, :]
                    if n == PT:
                        src, dst = (x.rearrange("p (b t) -> p b t", b=DB) for x in (src, dst))
                        b = bs[:, k, 0:DT].unsqueeze(1).to_broadcast([P, DB, DT])
                    ins = dve.tensor_tensor(dst, src, b, ALU.add)
                ins.then_inc(gate_add, 1)
                dve.wait_ge(gate_add, n + 1)
                dve.tensor_tensor(c.mT[:, 6:8, cols(n)], c.mT[:, 6:8, cols(n)], gate_p[:, n % 2, :, 0:m], ALU.mult).then_inc(gate_done, 1)
            dve.wait_ge(state_turned, 1)
            dve.tensor_copy(state_t[:, :], ps[:NST, 3, 0:GW]).then_inc(state_copied, 1)


def index_prompt(c, st):
    nc, io, ps = c.nc, c.io, c.ps
    sb = lambda name, shape: c.sb(name, shape, stack=st)
    causal = sb("causal", [P, P])
    relu = sb("index_relu", [P, 2, 4, 512])
    score = sb("index_score", [P, 2, SEQ])
    top = sb("top8", [P, 8])
    s = c.layer_sem
    in_, heads_done, relud, relu_used = s("ix_in"), s("ix_heads"), s("ix_relu"), s("ix_relu_used")
    part, scored, top_found, taken, mask_done = s("ix_part"), s("ix_scored"), s("ix_top"), s("ix_taken"), s("ix_mask")
    items = [(n, a, min(512, (n + 1) * P - a)) for n in range(PT) for a in range(0, (n + 1) * P, 512)]

    with nc.Block() as block:
        @block.sync
        def _(sp):
            sp.dma_start(causal[:, :], io["causal"]).then_inc(in_, 16)

        @block.tensor
        def _(pe):
            for i, (n, a, w) in enumerate(items):
                if i >= 2:
                    pe.wait_ge(relud, i - 1)
                for h in range(IXH):
                    ins = pe.matmul(ps[:, 4 * (i % 2) + h, 0:w], c.qiT[32 * h:32 * h + 32, cols(n)],
                                    c.kiT[32 * h:32 * h + 32, a:a + w], start=True, stop=True)
                ins.then_inc(heads_done, 1)

        @block.scalar
        def _(act):
            for i, (n, a, w) in enumerate(items):
                act.wait_ge(heads_done, i + 1)
                if i >= 2:
                    act.wait_ge(relu_used, i - 1)
                for h in range(IXH):
                    ins = act.activation(relu[:, i % 2, h, 0:w], ps[:, 4 * (i % 2) + h, 0:w], ACT.Relu)
                ins.then_inc(relud, 1)

        @block.vector
        def _(dve):
            np_, nt = 0, 0
            dve.wait_ge(in_, 16)
            for i, (n, a, w) in enumerate(items):
                I = score[:, n % 2, :]
                dve.wait_ge(relud, i + 1)
                dve.tensor_scalar(I[:, a:a + w], relu[:, i % 2, 0, 0:w], c.wi[:, n, 0:1], None, ALU.mult).then_inc(part, 1)
                np_ += 1
                for h in range(1, IXH):
                    dve.wait_ge(part, np_)
                    ins = dve.scalar_tensor_tensor(out=I[:, a:a + w], in0=relu[:, i % 2, h, 0:w], scalar=c.wi[:, n, h:h + 1],
                                                   in1=I[:, a:a + w], op0=ALU.mult, op1=ALU.add)
                    if h < IXH - 1:
                        ins.then_inc(part, 1)
                        np_ += 1
                    else:
                        ins.then_inc(relu_used, 1)
                dve.wait_ge(relu_used, i + 1)
                if a + w < (n + 1) * P:
                    continue
                N = (n + 1) * P
                if n < TOPK // P:
                    m = c.mask_c[:, mask_at(n)]
                    if n:
                        dve.memset(m[:, 0:n * P], 0.0)
                    dve.tensor_copy(m[:, n * P:], causal[:, :]).then_inc(mask_done, 1)
                    continue
                dve.tensor_tensor(I[:, n * P:N], I[:, n * P:N], causal[:, :], ALU.add).then_inc(scored, 1)
                dve.wait_ge(scored, n - TOPK // P + 1)
                for _ in range(TOPK // 8):
                    dve.max(top[:, :], I[:, 0:N]).then_inc(top_found, 1)
                    nt += 1
                    dve.wait_ge(top_found, nt)
                    dve.match_replace(I[:, 0:N], top[:, :], I[:, 0:N], TAKEN).then_inc(taken, 1)
                    dve.wait_ge(taken, nt)
                dve.tensor_scalar(c.mask_c[:, mask_at(n)], I[:, 0:N], TAKEN, NEG, ALU.is_gt, ALU.mult).then_inc(mask_done, 1)


def attend_prompt(c, st):
    nc, io, ps = c.nc, c.io, c.ps
    sb = lambda name, shape, dt=F32: c.sb(name, shape, dt, stack=st)
    bias_b = sb("bias_b", [P, SEQ])
    S = sb("scores", [P, 2, SEQ])
    PTs = sb("probs_t", [P, 2, PT, P])
    O = sb("out_tok", [P, 2, GW])
    mx, sm, rs = sb("row_max", [P, 2]), sb("row_sum", [P, 2]), sb("row_inv", [P, 2])
    s = c.layer_sem
    in_, scored, biased, maxed, exped, turned, unloaded, pv_done, inv_done, out_done, o_turned, o_copied, s_freed = (
        s(f"at_{n}") for n in ("in", "scored", "biased", "maxed", "exped", "turned", "unloaded", "pv", "inv", "out", "o_turned", "o_copied", "s_freed"))
    jobs = [(x, n, h) for x in "bc" for n in range(PT) for h in range(NH)]
    batches = [(j, a, min(4, n + 1 - a)) for j, (x, n, h) in enumerate(jobs) for a in range(0, n + 1, 4)]
    of_job = [[b for b, (jj, _, _) in enumerate(batches) if jj == j] for j in range(len(jobs))]
    J = len(jobs)

    with nc.Block() as block:
        @block.sync
        def _(sp):
            sp.dma_start(bias_b[:, :], io["bias_b"]).then_inc(in_, 16)

        @block.tensor
        def _(pe):
            def score(j):
                x, n, h = jobs[j]
                if j >= 2:
                    pe.wait_ge(biased, j - 1)
                r = 64 * (h % 2)
                N = (n + 1) * P
                for a in range(0, N, 512):
                    w = min(512, N - a)
                    ins = pe.matmul(ps[:, 2 * (j % 2) + a // 512, 0:w], c.mT[r:r + 64, c.chunk[x] + h // 2, cols(n)],
                                    c.kT[x][r:r + 64, h // 2, a:a + w], start=True, stop=True)
                ins.then_inc(scored, 1)

            def turn(j):
                pe.wait_ge(exped, j + 1)
                for b in of_job[j]:
                    _, a, nb = batches[b]
                    if b >= 2:
                        pe.wait_ge(unloaded, b - 1)
                    for q in range(nb):
                        ins = pe.transpose(ps[:, 4 + b % 2, q * P:(q + 1) * P], S[:, j % 2, (a + q) * P:(a + q + 1) * P], c.ident[:, :])
                    ins.then_inc(turned, 1)

            def values(j):
                x, n, h = jobs[j]
                pe.wait_ge(unloaded, of_job[j][-1] + 1)
                if j >= 1:
                    pe.wait_ge(out_done, j)
                for q in range(n + 1):
                    ins = pe.matmul(ps[:, 6, h * HD:(h + 1) * HD], PTs[:, j % 2, q, :], c.v[x][:, q, h * HD:(h + 1) * HD],
                                    start=(q == 0), stop=(q == n))
                ins.then_inc(pv_done, 1)

            def turn_out(t):
                pe.wait_ge(out_done, NH * (t + 1))
                if t >= 1:
                    pe.wait_ge(o_copied, t)
                for k in range(2):
                    ins = pe.transpose(ps[:, 7, k * P:(k + 1) * P], O[:, t % 2, k * P:(k + 1) * P], c.ident[:, :])
                ins.then_inc(o_turned, 1)

            for j in range(J + 2):
                if j < J:
                    score(j)
                if 1 <= j <= J:
                    turn(j - 1)
                if j >= 2:
                    values(j - 2)
                    if (j - 2) % NH == 0 and j - 2 > 0:
                        turn_out((j - 2) // NH - 1)
            turn_out(J // NH - 1)

        @block.scalar
        def _(act):
            def unload(j):
                for b in of_job[j]:
                    _, a, nb = batches[b]
                    act.wait_ge(turned, b + 1)
                    if j >= 2:
                        act.wait_ge(pv_done, j - 1)
                    act.activation(PTs[:, j % 2, a:a + nb, :].rearrange("p b t -> p (b t)"), ps[:, 4 + b % 2, 0:nb * P], ACT.Copy).then_inc(unloaded, 1)

            for j in range(J + 1):
                if j < J:
                    x, n, h = jobs[j]
                    act.wait_ge(maxed, j + 1)
                    if j >= 2:
                        act.wait_ge(inv_done, j - 1)
                    act.activation(S[:, j % 2, 0:(n + 1) * P], S[:, j % 2, 0:(n + 1) * P], ACT.Exp, bias=mx[:, j % 2:j % 2 + 1],
                                   accum_out=sm[:, j % 2:j % 2 + 1]).then_inc(exped, 1)
                if j >= 1:
                    unload(j - 1)

        @block.vector
        def _(dve):
            def norm_out(j):
                x, n, h = jobs[j]
                dve.wait_ge(exped, j + 1)
                dve.reciprocal(rs[:, j % 2:j % 2 + 1], sm[:, j % 2:j % 2 + 1]).then_inc(inv_done, 1)
                dve.wait_ge(inv_done, j + 1)
                dve.wait_ge(pv_done, j + 1)
                if h == 0 and j >= 2 * NH:
                    dve.wait_ge(o_turned, j // NH - 1)
                dve.tensor_scalar(O[:, (j // NH) % 2, h * HD:(h + 1) * HD], ps[:, 6, h * HD:(h + 1) * HD], rs[:, j % 2:j % 2 + 1],
                                  None, ALU.mult).then_inc(out_done, 1)

            def copy_out(t):
                x, n, _ = jobs[t * NH]
                dve.wait_ge(o_turned, t + 1)
                dve.tensor_copy(c.mT[:, c.chunk[x]:c.chunk[x] + 2, cols(n)],
                                ps[:, 7, 0:GW].rearrange("p (k t) -> p k t", k=2)).then_inc(o_copied, 1)

            dve.wait_ge(in_, 16)
            for j in range(J + 2):
                if j < J:
                    x, n, h = jobs[j]
                    N = (n + 1) * P
                    dve.wait_ge(scored, j + 1)
                    if j >= 2:
                        dve.wait_ge(turned, of_job[j - 2][-1] + 1)
                    bias = bias_b[:, SEQ - N:SEQ] if x == "b" else c.mask_c[:, mask_at(n)]
                    dve.scalar_tensor_tensor(out=S[:, j % 2, 0:N], in0=ps[:, 2 * (j % 2):2 * (j % 2) + 2, :].rearrange("p b t -> p (b t)")[:, 0:N],
                                             scalar=SCALE, in1=bias, op0=ALU.mult, op1=ALU.add).then_inc(biased, 1)
                    dve.wait_ge(biased, j + 1)
                    dve.tensor_reduce(mx[:, j % 2:j % 2 + 1], S[:, j % 2, 0:N], AX.X, ALU.max, negate=True).then_inc(maxed, 1)
                if j >= 2:
                    norm_out(j - 2)
                    if (j - 2) % NH == 1 and j - 2 > NH:
                        copy_out((j - 2) // NH - 1)
            copy_out(J // NH - 1)


def attend_sample(c, st):
    nc, io, ps, l = c.nc, c.io, c.ps, c.l
    sb = lambda name, shape, dt=F32: c.sb(name, shape, dt, stack=st)
    flat, used = c.hT[:, :, :].rearrange("p k t -> p (k t)"), [0]

    def of_h(*dims):
        a = used[0]
        used[0] += int(np.prod(dims))
        assert used[0] <= KC * T
        names = "abc"[:len(dims)]
        return flat[:, a:used[0]].rearrange(f"p ({' '.join(names)}) -> p {' '.join(names)}", **dict(zip(names, dims)))

    own = of_h(DB, P)
    rep_heads, sum_heads, new_ok = sb("rep_heads", [NS, P]), sb("sum_heads", [P, NS]), sb("new_ok", [NS, NS])
    bias_sb = sb("bias_sb", [P, BT * P + NS])
    qf = sb("q_rows", [P, 2, P])
    qz = of_h(2, DB, P)
    ixf, ixz = sb("ixq_rows", [P, P]), of_h(DB, P)
    qi4 = sb("ixq_tok", [NS, 4, 4, IXD])
    w_rows, w_cols = sb("wi_rows", [P, 4]), sb("wi_col", [P, 1])
    ki_in = of_h(DB, P)
    ki_t = of_h(DB, P)
    R = sb("ix_relu_s", [P, 512])
    I = sb("ix_score_s", [NS, PAST + NS])
    top = sb("top8_s", [NS, 8])
    kin = sb("k_in", [P, 3, 4, GW])
    kt = c.acT.rearrange("p k t -> p (k t)")[:, 0:2048].rearrange("p (i a t) -> p i a t", i=2, a=2)
    S = of_h(PAST + NS)
    PTs = sb("probs_s_t", [P, PAGES + 1, P])
    VP = 8
    vin = sb("v_in", [P, 2, VP, GW])
    mx, sm, rs = sb("max_s", [P, 1]), sb("sum_s", [P, 1]), sb("inv_s", [P, 1])
    s = c.layer_sem
    names = ("const", "qi4", "ixq_turned", "ixf", "ixz", "w_up", "w_rows", "w_col", "ki_turned", "ki_copied", "ix_heads",
             "ix_relu", "ix_sum", "ix_copied", "ix_mask_add", "top", "taken", "mask", "qf", "qz", "k_turned", "k_copied",
             "qk", "masked", "new_keys", "s_copied", "max", "exp", "inv", "norm", "p_turned", "p_copied", "pv", "out")
    q = {n: s(f"sm_{n}") for n in names}
    ki_sem = s("sm_ki_in")
    ki_used = s("sm_ki_used")
    k_sem = [s(f"sm_k_in{i}") for i in range(3)]
    v_sem = [s(f"sm_v_in{i}") for i in range(2)]
    scol = slice(SEQ, T)
    page_keys = io["cache_kidx_c"][l].rearrange("g (j c) d -> g j (c d)", c=4)
    pool = {"k": io["cache_k_c"][l].rearrange("g s h d -> g s (h d)"), "v": io["cache_v_c"][l].rearrange("g s h d -> g s (h d)")}
    win = {"k": io["cache_k_b"][l].rearrange("b s h d -> b s (h d)"), "v": io["cache_v_b"][l].rearrange("b s h d -> b s (h d)")}
    chunks = {"b": [(0, 4), (4, BT - 4)], "c": [(4 * i, 4) for i in range(CT // 4)]}
    kitems = [(x, ci, a, nt, b) for x in "cb" for ci, (a, nt) in enumerate(chunks[x]) for b in range(DB)]
    vitems = {"c": [(b, a, VP) for b in range(DB) for a in range(0, CT, VP)], "b": [(b, 0, BT) for b in range(DB)]}
    vall = [("c", *v) for v in vitems["c"]] + [("b", *v) for v in vitems["b"]]

    def window_tile(dst, which, b, t):
        if t < FAR_TILES:
            src = win[which][b, t * 16 * (P // DT):(t + 1) * 16 * (P // DT), :].rearrange("(g r) n -> g r n", r=16)[:, 0:DT, :]
            return dst, src
        a = PAST - 512 + (t - FAR_TILES) * P
        return dst, win[which][b, a:a + P, :]

    kat, vat = [], []
    cnt = [0] * 3
    for i, (x, ci, a, nt, b) in enumerate(kitems):
        cnt[i % 3] += 16 * nt
        kat.append(cnt[i % 3])
    cnt = [0] * 2
    for i, (x, b, a, nt) in enumerate(vall):
        cnt[i % 2] += 16 * nt
        vat.append(cnt[i % 2])
    VOFF = len(vitems["c"])
    HC, NC_ = PAST // 512, len(kitems)

    with nc.Block() as block:
        @block.sync
        def _(sp):
            for dst, name in ((own[:, :, :].rearrange("p b t -> p (b t)"), "own_col"), (rep_heads[:, :], "rep_heads"), (sum_heads[:, :], "sum_heads"),
                              (new_ok[:, :], "new_ok"), (bias_sb[:, :], "bias_sb")):
                sp.dma_start(dst, io[name]).then_inc(q["const"], 16)
            for ch in range(HC):
                if ch >= 1:
                    sp.wait_ge(q["ki_turned"], 2 * ch)
                for b in range(DB):
                    for p_ in range(4):
                        i = b * PAGES + 4 * ch + p_
                        page = sp.value_load(c.tables[0:1, i:i + 1], min_val=0, max_val=POOL_PAGES - 1)
                        sp.dma_start(ki_in[32 * p_:32 * p_ + 32, b, :], page_keys[page]).then_inc(ki_sem, 16)

            def load_k(i):
                x, ci, a, nt, b = kitems[i]
                if i >= 3:
                    sp.wait_ge(q["k_turned"], 2 * (i - 2))
                for t in range(nt):
                    dst = kin[:, i % 3, t, :]
                    if x == "c":
                        page = sp.value_load(c.tables[0:1, b * PAGES + a + t:b * PAGES + a + t + 1], min_val=0, max_val=POOL_PAGES - 1)
                        sp.dma_start(dst, pool["k"][page]).then_inc(k_sem[i % 3], 16)
                    else:
                        d_, s_ = window_tile(dst, "k", b, a + t)
                        sp.dma_start(d_, s_).then_inc(k_sem[i % 3], 16)

            def load_v(i):
                x, b, a, nt = vall[i]
                if i >= 2:
                    sp.wait_ge(q["pv"], i - 1)
                for t in range(nt):
                    dst = vin[:, i % 2, t, :]
                    if x == "c":
                        page = sp.value_load(c.tables[0:1, b * PAGES + a + t:b * PAGES + a + t + 1], min_val=0, max_val=POOL_PAGES - 1)
                        sp.dma_start(dst, pool["v"][page]).then_inc(v_sem[i % 2], 16)
                    else:
                        d_, s_ = window_tile(dst, "v", b, a + t)
                        sp.dma_start(d_, s_).then_inc(v_sem[i % 2], 16)

            nkc = sum(1 for k in kitems if k[0] == "c")
            for i in range(nkc):
                load_k(i)
            load_v(0)
            load_v(1)
            for i in range(2, VOFF):
                load_v(i)
            for i in range(nkc, len(kitems)):
                load_k(i)
            for i in range(VOFF, len(vall)):
                load_v(i)

        @block.tensor
        def _(pe):
            pe.wait_ge(q["qi4"], 1)
            for h in range(IXH):
                ins = pe.transpose(ps[:, 0, h * NS:(h + 1) * NS], qi4[:, h, :, :].rearrange("p r d -> p (r d)"), c.ident[:NS, :NS])
            ins.then_inc(q["ixq_turned"], 1)
            pe.wait_ge(q["const"], 80)
            pe.matmul(ps[:, 1, 0:IXH], rep_heads[:, :], c.wi[:NS, PT, :], start=True, stop=True).then_inc(q["w_up"], 1)
            pe.wait_ge(q["ixz"], 1)
            for ch in range(HC):
                pe.wait_ge(ki_sem, 16 * 4 * DB * (ch + 1))
                for half in range(2):
                    i = 2 * ch + half
                    if i >= 1:
                        pe.wait_ge(q["ki_copied"], i)
                    for b in range(4):
                        ins = pe.transpose(ps[:, 2, b * P:(b + 1) * P], ki_in[:, 4 * half + b, :], c.ident[:, :])
                    ins.then_inc(q["ki_turned"], 1)
                pe.wait_ge(q["ki_copied"], 2 * (ch + 1))
                if ch >= 1:
                    pe.wait_ge(q["ix_relu"], ch)
                for r in range(4):
                    for b in range(DB):
                        ins = pe.matmul(ps[:, 4 + r, 0:P], ixz[32 * r:32 * r + 32, b, :], ki_t[32 * r:32 * r + 32, b, :],
                                        start=(b == 0), stop=(b == DB - 1))
                ins.then_inc(q["ix_heads"], 1)
                pe.wait_ge(q["ix_relu"], ch + 1)
                if ch >= 1:
                    pe.wait_ge(q["ix_copied"], ch)
                pe.matmul(ps[:NS, 3, :], sum_heads[:, :], R[:, :], start=True, stop=True).then_inc(q["ix_sum"], 1)
            pe.matmul(ps[:, 4, 0:NS], ixf[0:32, :], c.kiT[0:32, scol], start=True, stop=True).then_inc(q["ix_heads"], 1)
            pe.wait_ge(q["ix_relu"], HC + 1)
            pe.wait_ge(q["ix_copied"], HC)
            pe.matmul(ps[:NS, 3, 0:NS], sum_heads[:, :], R[:, 0:NS], start=True, stop=True).then_inc(q["ix_sum"], 1)

            pe.wait_ge(q["ix_copied"], HC + 1)
            si = 0
            nki = 0
            for xi, x in enumerate("cb"):
                pe.wait_ge(q["qz"], 2 * (xi + 1))
                for ci, (a, nt) in enumerate(chunks[x]):
                    sbank = si % 2
                    if si >= 2:
                        pe.wait_ge(q["s_copied"], si - 1)
                    for b in range(DB):
                        i = nki
                        pe.wait_ge(k_sem[i % 3], kat[i])
                        for hp in range(2):
                            if i >= 1:
                                pe.wait_ge(q["k_copied"], 2 * (i - 1) + hp + 1)
                            for t in range(nt):
                                ins = pe.transpose(ps[:, 2 + hp, t * P:(t + 1) * P], kin[:, i % 3, t, hp * P:(hp + 1) * P], c.ident[:, :])
                            ins.then_inc(q["k_turned"], 1)
                        for hp in range(2):
                            pe.wait_ge(q["k_copied"], 2 * i + hp + 1)
                            ins = pe.matmul(ps[:, sbank, 0:nt * P], qz[:, hp, b, :], kt[:, i % 2, hp, 0:nt * P],
                                            start=(b == 0 and hp == 0), stop=(x == "b" and b == DB - 1 and hp == 1))
                        ins.then_inc(q["qk"], 1)
                        if x == "c" and b == DB - 1:
                            pe.wait_ge(q["mask"], 1)
                            pe.matmul(ps[:, sbank, 0:512], rep_heads[:, :], I[:, ci * 512:(ci + 1) * 512],
                                      start=False, stop=True).then_inc(q["masked"], 1)
                        nki += 1
                    si += 1
                if si >= 2:
                    pe.wait_ge(q["s_copied"], si - 1)
                for hp in range(2):
                    ins = pe.matmul(ps[:, si % 2, 0:NS], qf[:, hp, :], c.kT[x][:, hp, scol], start=(hp == 0), stop=(hp == 1 and x == "b"))
                if x == "c":
                    ins = pe.matmul(ps[:, si % 2, 0:NS], rep_heads[:, :], I[:, PAST:PAST + NS], start=False, stop=True)
                ins.then_inc(q["new_keys"], 1)
                si += 1
                tiles = CT if x == "c" else BT
                pe.wait_ge(q["norm"], xi + 1)
                for bt in range((tiles + 3) // 4 + 1):
                    gi = bt + (0 if x == "c" else CT // 4 + 1)
                    if gi >= 2:
                        pe.wait_ge(q["p_copied"], gi - 1)
                    if bt == (tiles + 3) // 4:
                        ins = pe.transpose(ps[:NS, 4 + gi % 2, 0:P], S[:, tiles * P:tiles * P + NS], c.ident[:, :])
                    else:
                        for t in range(min(4, tiles - 4 * bt)):
                            ins = pe.transpose(ps[:, 4 + gi % 2, t * P:(t + 1) * P], S[:, (4 * bt + t) * P:(4 * bt + t + 1) * P], c.ident[:, :])
                    ins.then_inc(q["p_turned"], 1)
                pe.wait_ge(q["p_copied"], CT // 4 + 1 if x == "c" else CT // 4 + 1 + (BT + 3) // 4 + 1)
                if xi == 1:
                    pe.wait_ge(q["out"], 4)
                for hp in range(2):
                    pe.matmul(ps[:, 6 + hp, 0:64], c.v[x][:NS, PT, hp * P:(hp + 1) * P], PTs[:NS, tiles, hp * 64:(hp + 1) * 64],
                              start=True, stop=False, skip_group_check=True)
                for vi, (b, a, nt) in enumerate(vitems[x]):
                    i = vi + (0 if x == "c" else VOFF)
                    pe.wait_ge(v_sem[i % 2], vat[i])
                    for t in range(nt):
                        for hp in range(2):
                            fin = vi == len(vitems[x]) - 1 and t == nt - 1
                            ins = pe.matmul(ps[:, 6 + hp, 0:64].rearrange("p (h r) -> p h r", h=2)[:, :, b * DT:(b + 1) * DT],
                                            vin[:, i % 2, t, hp * P:(hp + 1) * P],
                                            PTs[:, a + t, hp * 64:(hp + 1) * 64].rearrange("p (h r) -> p h r", h=2)[:, :, b * DT:(b + 1) * DT],
                                            start=False, stop=fin, skip_group_check=True)
                    ins.then_inc(q["pv"], 1)

        @block.scalar
        def _(act):
            def exps(xi):
                N = (CT if xi == 0 else BT) * P + NS
                act.wait_ge(q["max"], xi + 1)
                act.activation(S[:, 0:N], S[:, 0:N], ACT.Exp, bias=mx[:, 0:1], accum_out=sm[:, 0:1]).then_inc(q["exp"], 1)

            for i in range(2 * HC):
                act.wait_ge(q["ki_turned"], i + 1)
                if i >= 2:
                    act.wait_ge(q["ix_heads"], i // 2)
                act.activation(ki_t[:, 4 * (i % 2):4 * (i % 2) + 4, :].rearrange("p b t -> p (b t)"), ps[:, 2, :], ACT.Copy).then_inc(q["ki_copied"], 1)
            for i, (x, ci, a, nt, b) in enumerate(kitems):
                if i >= 2:
                    act.wait_ge(q["qk"], i - 1)
                for hp in range(2):
                    act.wait_ge(q["k_turned"], 2 * i + hp + 1)
                    act.activation(kt[:, i % 2, hp, 0:nt * P], ps[:, 2 + hp, 0:nt * P], ACT.Copy).then_inc(q["k_copied"], 1)
                if i == CT // 4 * DB - 1:
                    exps(0)
            exps(1)

        @block.vector
        def _(dve):
            dve.tensor_copy(qi4[:, :, :, :], c.qi_tok[:, :].rearrange("p (h d) -> p h d", h=IXH).unsqueeze(2).to_broadcast([NS, 4, 4, IXD])).then_inc(q["qi4"], 1)
            dve.wait_ge(q["const"], 80)
            dve.wait_ge(q["ixq_turned"], 1)
            dve.tensor_copy(ixf[:, :], ps[:, 0, 0:P]).then_inc(q["ixf"], 1)
            dve.wait_ge(q["ixf"], 1)
            dve.tensor_tensor(ixz[:, :, :], ixf[:, :].unsqueeze(1).to_broadcast([P, DB, P]), own[:, :, :], ALU.mult).then_inc(q["ixz"], 1)
            dve.wait_ge(q["w_up"], 1)
            for h in range(IXH):
                ins = dve.tensor_copy(w_cols[32 * h:32 * h + 32, :], ps[32 * h:32 * h + 32, 1, h:h + 1])
            ins.then_inc(q["w_col"], 1)
            dve.wait_ge(q["w_col"], 1)
            for ch in range(HC):
                dve.wait_ge(q["ix_heads"], ch + 1)
                if ch >= 1:
                    dve.wait_ge(q["ix_sum"], ch)
                for r in range(4):
                    ins = dve.tensor_scalar(R[:, :].rearrange("p (g j r) -> p g j r", g=4, r=4)[:, :, :, r],
                                            ps[:, 4 + r, 0:P].rearrange("p (g j) -> p g j", g=4), 0.0, w_cols[:, 0:1], ALU.max, ALU.mult)
                ins.then_inc(q["ix_relu"], 1)
                dve.wait_ge(q["ix_sum"], ch + 1)
                dve.tensor_copy(I[:, ch * 512:(ch + 1) * 512], ps[:NS, 3, :]).then_inc(q["ix_copied"], 1)
            dve.wait_ge(q["ix_heads"], HC + 1)
            dve.tensor_scalar(R[:, 0:NS], ps[:, 4, 0:NS], 0.0, w_cols[:, 0:1], ALU.max, ALU.mult).then_inc(q["ix_relu"], 1)
            dve.wait_ge(q["ix_sum"], HC + 1)
            dve.tensor_tensor(I[:, PAST:], ps[:NS, 3, 0:NS], new_ok[:, :], ALU.add).then_inc(q["ix_copied"], 1)
            dve.wait_ge(q["ix_copied"], HC + 1)
            for i in range(TOPK // 8):
                dve.max(top[:, :], I[:, :]).then_inc(q["top"], 1)
                dve.wait_ge(q["top"], i + 1)
                dve.match_replace(I[:, :], top[:, :], I[:, :], TAKEN).then_inc(q["taken"], 1)
                dve.wait_ge(q["taken"], i + 1)
            dve.tensor_scalar(I[:, :], I[:, :], TAKEN, NEG, ALU.is_gt, ALU.mult).then_inc(q["mask"], 1)

            si, gi = 0, 0
            for xi, x in enumerate("cb"):
                if xi:
                    dve.wait_ge(q["new_keys"], 1)
                dve.memset(qf[:, :, :], 0.0).then_inc(q["qf"], 1)
                dve.wait_ge(q["qf"], 3 * xi + 1)
                for hp in range(2):
                    for hl in range(2):
                        h = 2 * hp + hl
                        ins = dve.tensor_copy(qf[64 * hl:64 * hl + 64, hp, h * NS:(h + 1) * NS],
                                              c.mT[64 * hl:64 * hl + 64, c.chunk[x] + hp, scol])
                    ins.then_inc(q["qf"], 1)
                dve.wait_ge(q["qf"], 3 * xi + 3)
                for hp in range(2):
                    dve.tensor_tensor(qz[:, hp, :, :], qf[:, hp, :].unsqueeze(1).to_broadcast([P, DB, P]), own[:, :, :], ALU.mult).then_inc(q["qz"], 1)
                for ci, (a, nt) in enumerate(chunks[x]):
                    if x == "c":
                        dve.wait_ge(q["masked"], ci + 1)
                        dve.tensor_scalar(S[:, a * P:(a + nt) * P], ps[:, si % 2, 0:nt * P], SCALE, None, ALU.mult).then_inc(q["s_copied"], 1)
                    else:
                        if ci == 0:
                            dve.wait_ge(q["p_turned"], CT // 4 + 1)
                        dve.wait_ge(q["qk"], DB * (CT // 4 + ci + 1))
                        dve.scalar_tensor_tensor(out=S[:, a * P:(a + nt) * P], in0=ps[:, si % 2, 0:nt * P], scalar=SCALE,
                                                 in1=bias_sb[:, a * P:(a + nt) * P], op0=ALU.mult, op1=ALU.add).then_inc(q["s_copied"], 1)
                    si += 1
                tiles = CT if x == "c" else BT
                N = tiles * P + NS
                dve.wait_ge(q["new_keys"], xi + 1)
                if x == "c":
                    dve.tensor_scalar(S[:, tiles * P:N], ps[:, si % 2, 0:NS], SCALE, None, ALU.mult).then_inc(q["s_copied"], 1)
                else:
                    dve.scalar_tensor_tensor(out=S[:, tiles * P:N], in0=ps[:, si % 2, 0:NS], scalar=SCALE, in1=bias_sb[:, tiles * P:N],
                                             op0=ALU.mult, op1=ALU.add).then_inc(q["s_copied"], 1)
                si += 1
                dve.wait_ge(q["s_copied"], si)
                dve.tensor_reduce(mx[:, :], S[:, 0:N], AX.X, ALU.max, negate=True).then_inc(q["max"], 1)
                dve.wait_ge(q["exp"], xi + 1)
                dve.reciprocal(rs[:, :], sm[:, :]).then_inc(q["inv"], 1)
                dve.wait_ge(q["inv"], xi + 1)
                dve.tensor_scalar(S[:, 0:N], S[:, 0:N], rs[:, 0:1], None, ALU.mult).then_inc(q["norm"], 1)
                if xi:
                    dve.wait_ge(q["pv"], VOFF)
                nb = (tiles + 3) // 4
                for bt in range(nb + 1):
                    dve.wait_ge(q["p_turned"], gi + 1)
                    if bt == nb:
                        ins = dve.tensor_copy(PTs[:NS, tiles, :], ps[:NS, 4 + gi % 2, 0:P])
                    else:
                        w = min(4, tiles - 4 * bt)
                        ins = dve.tensor_copy(PTs[:, 4 * bt:4 * bt + w, :].rearrange("p b t -> p (b t)"), ps[:, 4 + gi % 2, 0:w * P])
                    ins.then_inc(q["p_copied"], 1)
                    gi += 1
                dve.wait_ge(q["pv"], VOFF if x == "c" else len(vall))
                for hp in range(2):
                    for hl in range(2):
                        dve.tensor_copy(c.mT[64 * hl:64 * hl + 64, c.chunk[x] + hp, scol],
                                        ps[64 * hl:64 * hl + 64, 6 + hp, hl * NS:(hl + 1) * NS]).then_inc(q["out"], 1)


def out_stage(c, st, name, w_dram, rhs, K, g_post, g_pre, x_from):
    nc, io, ps, l, xT, oT = c.nc, c.io, c.ps, c.l, c.xT, c.hT
    sb = lambda n, shape: c.sb(f"{name}_{n}", shape, stack=st)
    SLOTS = 3 if K <= KC else 2
    W = sb("w", [P, SLOTS, K, P])
    sq, acc, rstd, g = sb("sq", [P, 2, T]), sb("acc", [P, T]), sb("rstd", [P, T]), sb("g", [P, 2, KC])
    s = lambda n: c.layer_sem(f"{name}_{n}")
    w_in = [s(f"w_in{i}") for i in range(SLOTS)]
    x_in, g_in, done, copied, squared, added, summed, rooted, inverted, scaled, x_done, x_sq, x_add, h_done, parked = (
        s(n) for n in ("x_in", "g_in", "done", "copied", "squared", "added", "summed", "rooted", "inverted", "scaled", "x_done",
                       "x_sq", "x_add", "h_done", "parked"))
    w_all = w_dram[l].rearrange("(k p) n -> p k n", p=P)
    banks = lambda d: ps[:, 3 * (d % 2):3 * (d % 2) + 3, 0:TH]
    by3 = lambda ap: ap.rearrange("p (a t) -> p a t", a=3)
    with nc.Block() as block:
        @block.sync
        def _(sp):
            if x_from is not None:
                sp.dma_start(xT[:, :, :].rearrange("p k t -> p (k t)"), x_from).then_inc(x_in, 16)
            sp.dma_start(g[:, 0, :], gain(io[g_post], l)).then_inc(g_in, 16)
            if g_pre:
                sp.dma_start(g[:, 1, :], gain(io[g_pre], l)).then_inc(g_in, 16)
            for d in range(KC):
                if d >= SLOTS:
                    sp.wait_ge(done, d - SLOTS + 1)
                sp.dma_start(W[:, d % SLOTS, :, :], w_all[:, :, d * P:(d + 1) * P]).then_inc(w_in[d % SLOTS], 16)
            if not g_pre:
                sp.wait_ge(x_done, KC)
                sp.dma_start(c.xpark, xT[:, :, :].rearrange("p k t -> p (k t)")).then_inc(parked, 16)
                sp.wait_ge(parked, 16)

        @block.tensor
        def _(pe):
            for d in range(KC):
                pe.wait_ge(w_in[d % SLOTS], 16 * (d // SLOTS + 1))
                if d >= 2:
                    pe.wait_ge(copied, d - 1)
                for k in range(K):
                    for th in range(3):
                        ins = pe.matmul(banks(d)[:, th, :], W[:, d % SLOTS, k, :], rhs[:, k, th * TH:(th + 1) * TH],
                                        start=(k == 0), stop=(k == K - 1))
                ins.then_inc(done, 1)
            for r in range(2 if g_pre else 1):
                pe.wait_ge(added if r == 0 else x_add, KC - 1)
                pe.wait_ge(copied, KC)
                if r:
                    pe.wait_ge(rooted, 1)
                for th in range(3):
                    ins = pe.matmul(ps[:, th, 0:TH], c.ones[:, :], acc[:, th * TH:(th + 1) * TH], start=True, stop=True)
                ins.then_inc(summed, 1)

        @block.scalar
        def _(act):
            for d in range(KC):
                act.wait_ge(copied, d + 1)
                if d >= 3:
                    act.wait_ge(added, d - 2)
                act.activation(acc[:, :] if d == 0 else sq[:, d % 2, :], oT[:, d, :], ACT.Square).then_inc(squared, 1)
            for r in range(2 if g_pre else 1):
                act.wait_ge(summed, r + 1)
                act.activation(by3(rstd[:, :]), ps[:, 0:3, 0:TH], ACT.Sqrt, bias=c.eps[:, 0:1], scale=1.0 / D).then_inc(rooted, 1)
                if r == 0 and g_pre:
                    for k in range(KC):
                        act.wait_ge(x_done, k + 1)
                        if k >= 3:
                            act.wait_ge(x_add, k - 2)
                        act.activation(acc[:, :] if k == 0 else sq[:, k % 2, :], xT[:, k, :], ACT.Square).then_inc(x_sq, 1)

        @block.gpsimd
        def _(pool):
            for a, b in ((squared, added), (x_sq, x_add))[:2 if g_pre else 1]:
                for k in range(1, KC):
                    pool.wait_ge(a, k + 1)
                    if k > 1:
                        pool.wait_ge(b, k - 1)
                    pool.tensor_tensor(acc[:, :], acc[:, :], sq[:, k % 2, :], ALU.add).then_inc(b, 1)

        @block.vector
        def _(dve):
            for d in range(KC):
                dve.wait_ge(done, d + 1)
                dve.tensor_copy(by3(oT[:, d, :]), banks(d)).then_inc(copied, 1)
            dve.wait_ge(rooted, 1)
            dve.reciprocal(rstd[:, :], rstd[:, :]).then_inc(inverted, 1)
            dve.wait_ge(inverted, 1)
            dve.wait_ge(g_in, 32 if g_pre else 16)
            if x_from is not None:
                dve.wait_ge(x_in, 16)
            for k in range(KC):
                dve.scalar_tensor_tensor(out=oT[:, k, :], in0=oT[:, k, :], scalar=g[:, 0, k:k + 1], in1=rstd[:, :],
                                         op0=ALU.mult, op1=ALU.mult).then_inc(scaled, 1)
                dve.wait_ge(scaled, k + 1)
                dve.tensor_tensor(xT[:, k, :], xT[:, k, :], oT[:, k, :], ALU.add).then_inc(x_done, 1)
            if g_pre:
                dve.wait_ge(rooted, 2)
                dve.reciprocal(rstd[:, :], rstd[:, :]).then_inc(inverted, 1)
                dve.wait_ge(inverted, 2)
                for k in range(KC):
                    dve.scalar_tensor_tensor(out=c.hT[:, k, :], in0=xT[:, k, :], scalar=g[:, 1, k:k + 1], in1=rstd[:, :],
                                             op0=ALU.mult, op1=ALU.mult).then_inc(h_done, 1)


def ffn_in(c, st, aT):
    nc, io, ps, l, hT = c.nc, c.io, c.ps, c.l, c.hT
    s = c.layer_sem
    w_in = [s(f"f_w_in{i}") for i in range(2)]
    g_done, u_done, silu_done, mul_done = (s(f"f_{n}") for n in ("gate", "up", "silu", "mul"))
    w_gate, w_up = (io[n][l].rearrange("(k p) n -> p k n", p=P) for n in ("w_gate", "w_up"))
    with ExitStack() as st2:
        W = c.sb("f_w", [P, 2, 2, KC, P], stack=st2)
        sg = c.sb("f_silu", [P, 2, 3, TH], stack=st2)
        with nc.Block() as block:
            @block.sync
            def _(sp):
                for f in range(FC):
                    if f >= 2:
                        sp.wait_ge(u_done, f - 1)
                    for i, w in enumerate((w_gate, w_up)):
                        sp.dma_start(W[:, f % 2, i, :, :], w[:, :, f * P:(f + 1) * P]).then_inc(w_in[f % 2], 16)

            @block.tensor
            def _(pe):
                for f in range(FC):
                    pe.wait_ge(w_in[f % 2], 32 * (f // 2 + 1))
                    for i, (freed, done) in enumerate(((silu_done, g_done), (mul_done, u_done))):
                        if f >= 1:
                            pe.wait_ge(freed, f)
                        for k in range(KC):
                            for th in range(3):
                                ins = pe.matmul(ps[:, 3 * i + th, 0:TH], W[:, f % 2, i, k, :], hT[:, k, th * TH:(th + 1) * TH],
                                                start=(k == 0), stop=(k == KC - 1))
                        ins.then_inc(done, 1)

            @block.scalar
            def _(act):
                for f in range(FC):
                    act.wait_ge(g_done, f + 1)
                    if f >= 2:
                        act.wait_ge(mul_done, f - 1)
                    act.activation(sg[:, f % 2, :, :], ps[:, 0:3, 0:TH], ACT.Silu).then_inc(silu_done, 1)

            @block.vector
            def _(dve):
                for f in range(FC):
                    dve.wait_ge(silu_done, f + 1)
                    dve.wait_ge(u_done, f + 1)
                    dve.tensor_tensor(aT[:, f, :].rearrange("p (a t) -> p a t", a=3), ps[:, 3:6, 0:TH], sg[:, f % 2, :, :],
                                      ALU.mult).then_inc(mul_done, 1)


_INS = ["x_prompt", "x_sample", "cache_conv_a", "cache_k_b", "cache_v_b", "cache_k_c", "cache_v_c", "cache_kidx_c", "page_table",
        "w_in", "conv_w_a", "ln_g_d", "ln_b_d", "w_s_d", "b_s_d", "w_o", "w_gate", "w_up", "w_down",
        "g_pre_mix", "g_post_mix", "g_pre_ffn", "g_post_ffn"]
_OUTS = [("y_prompt", (1, SEQ, D)), ("y_sample", (DB, DT, D)), ("p_conv_a", (DEPTH, 1, 2, GW)),
         ("p_k_b", (DEPTH, 1, SEQ, NH, HD)), ("p_v_b", (DEPTH, 1, SEQ, NH, HD)),
         ("p_k_c", (DEPTH, 1, SEQ, NH, HD)), ("p_v_c", (DEPTH, 1, SEQ, NH, HD)), ("p_kidx_c", (DEPTH, 1, SEQ, IXD)),
         ("s_conv_a", (DEPTH, DB, 2, GW)), ("s_k_b", (DEPTH, DB, DT, NH, HD)), ("s_v_b", (DEPTH, DB, DT, NH, HD)),
         ("s_k_c", (DEPTH, DB, DT, NH, HD)), ("s_v_c", (DEPTH, DB, DT, NH, HD)), ("s_kidx_c", (DEPTH, DB, DT, IXD)),
         ("s_v_d", (DEPTH, DB, DT, GW))]


def build(nc, shapes):
    io = {n: nc.dram_tensor(f"in_{n}", sh, dt, kind="ExternalInput").ap() for n, (sh, dt) in shapes.items()}
    for n, sh in _OUTS:
        io[n] = nc.dram_tensor(f"out_{n}", sh, F32, kind="ExternalOutput").ap()
    program(nc, io)


def kernel(**inputs):
    import concourse.bacc as _bacc
    from concourse.bass_utils import run_bass_kernel_spmd as _run

    nc = _bacc.Bacc("TRN2", target_bir_lowering=False, num_devices=1)
    arrays = {n: np.ascontiguousarray(inputs[n]) for n in _INS}
    arrays.update(CONST)
    build(nc, {n: (a.shape, mybir.dt.from_np(a.dtype)) for n, a in arrays.items()})
    r = _run(nc, [{f"in_{n}": a for n, a in arrays.items()}], core_ids=[0])
    return tuple(r.results[0][f"out_{n}"] for n, _ in _OUTS)
```

```python
from contextlib import ExitStack, contextmanager

import numpy as np
import concourse.bass as bass
from concourse import mybir

ALU = mybir.AluOpType
ACT = mybir.ActivationFunctionType
AX = mybir.AxisListType
F32 = mybir.dt.float32
BF16 = mybir.dt.bfloat16
I32 = mybir.dt.int32
F32R = mybir.dt.float32r

P = 128
D = 1024
DEPTH = 2
SEQ = 1024
DB, DT = 8, 4
PAST = 2048
PAGE = 128
PAGES = PAST // PAGE
POOL_PAGES = 5 * DB * PAGES // 4
GW = 256
NH, HD = 4, 64
IXH, IXD = 4, 32
TOPK = 256
FF = 2816
EPS = 1e-6
SCALE = HD ** -0.5
THETA = 500000.0
NEG = -1e30
TAKEN = -3e38

KC = D // P
FC = FF // P
NS = DB * DT
TILES = SEQ // P + 1
PT = SEQ // P
T = SEQ + NS
TH = T // 3
NBANK = 8

C_AH, C_AB, C_AC, C_BQ, C_BK, C_BV, C_CQ, C_CK, C_CV = (i * GW for i in range(9))
C_IX = 9 * GW
IXW = IXH * IXD + IXD + IXH
C_DU = C_IX + IXW
C_DV = C_DU + GW
PROJ = C_DV + GW

FAR_TILES = (PAST - 512) // 16 * DT // P
NEAR_TILES = 512 // P
BT = FAR_TILES + NEAR_TILES
CT = PAGES


def tok(n):
    return P if n < PT else NS


def cols(n):
    return slice(n * P, n * P + tok(n))


def log_count(gap):
    m = np.zeros(gap.shape, np.float32)
    for window, dil in ((128, 1), (512, 4), (2048, 16)):
        m += (gap >= 0) & (gap <= window) & (gap % dil == 0)
    return np.where(m > 0, np.log(np.maximum(m, 1)), NEG).astype(np.float32)


def constants():
    i = np.arange(P)
    out = {}
    out["ident"] = np.eye(P, dtype=np.float32)
    out["bias_b"] = log_count(SEQ - P + i[:, None] - np.arange(SEQ)[None, :])
    out["causal"] = np.where(i[None, :] <= i[:, None], 0, NEG).astype(np.float32)
    out["tril_t"] = (i[:, None] <= i[None, :]).astype(np.float32)
    r = np.arange(NS)
    b, t = r // DT, r % DT
    hb, ht = np.tile(b, NH), np.tile(t, NH)
    far = np.arange(FAR_TILES * P)
    far = far // DT * 16 + far % DT
    near = PAST - 512 + np.arange(512)
    key = np.concatenate([far, near])
    own = hb[:, None] == b[None, :]
    new = np.where(own, log_count(np.where(own, ht[:, None] - t[None, :], -1)), NEG)
    out["bias_sb"] = np.concatenate([log_count(PAST + ht[:, None] - key[None, :]), new], 1).astype(np.float32)
    see = (b[:, None] == b[None, :]) & (t[None, :] <= t[:, None])
    out["new_ok"] = np.where(see, 0, NEG).astype(np.float32)
    out["own_col"] = np.tile((b[None, :] == np.arange(DB)[:, None]).astype(np.float32)[:, None, :],
                             (1, NH, 1)).reshape(1, DB * P).repeat(P, 0)
    out["rep_heads"] = np.tile(np.eye(NS, dtype=np.float32), (1, NH))
    out["sum_heads"] = out["rep_heads"].T.copy()
    out["rep_step"] = (np.arange(DT)[:, None] == t[None, :]).astype(np.float32)
    out["own_step"] = ((b[:, None] == b[None, :]) & (t[:, None] <= t[None, :])).astype(np.float32)

    pos = np.zeros((TILES, P), np.float32)
    pos[:PT] = np.arange(SEQ).reshape(PT, P)
    pos[PT, :NS] = PAST + t
    for name, half in (("rope_h", HD // 8), ("rope_i", IXD // 8)):
        inv = np.float32(THETA) ** (-np.arange(half, dtype=np.float32) / np.float32(half))
        ang = pos[:, :, None] * inv[None, None, :].astype(np.float32)
        c, s = np.cos(ang), np.sin(ang)
        tab = np.concatenate([c, c, -s, s], -1)
        out[name] = np.ascontiguousarray(tab.transpose(1, 0, 2).reshape(P, -1)).astype(np.float32)
    return out


CONST = constants()


def small(nc, why="small or strided by nature"):
    return nc.allow_non_contiguous_dma(reason=why)


class Shared:
    pass


def program(nc, io):
    nc.disable_value_cache = True
    with ExitStack() as es:
        es.enter_context(small(nc))
        c = Shared()
        c.nc, c.io = nc, io

        def sb(name, shape, dt=F32, stack=es):
            return stack.enter_context(nc.sbuf_tensor(name, shape, dt))

        def sem(name):
            s = es.enter_context(nc.semaphore(name))
            return s

        @contextmanager
        def phase():
            with ExitStack() as st:
                c.phase_sems = []
                c.layer_sem = lambda name: c.phase_sems.append(st.enter_context(nc.semaphore(name))) or c.phase_sems[-1]
                yield st
                for s in c.phase_sems:
                    nc.sync.sem_clear(s)
                nc.all_engine_barrier()

        c.sb = sb
        c.ps = es.enter_context(nc.psum_tensor("ps", [P, NBANK, 512], F32))
        c.xpark = nc.dram_tensor("xpark", (P, KC * T), F32, kind="Internal").ap()
        c.ident = sb("ident", [P, P])
        c.ones = sb("ones", [P, P])
        c.eps = sb("eps", [P, 1])
        c.rope_h = sb("rope_h", [P, TILES, HD // 2])
        c.rope_i = sb("rope_i", [P, TILES, IXD // 2])
        c.tables = sb("tables", [1, DB * PAGES], I32)
        c.xT = sb("xT", [P, KC, T])
        c.act_at = nc.sbuf_base
        c.act_hi = sb("act_hi", [P, KC, T], F32R)
        c.hT = nc.alloc_sbuf_tensor_at("hT", [P, KC, T], F32, offset=c.act_at)
        c.m_at = nc.sbuf_base
        c.mT = sb("mT", [P, KC, T])
        with ExitStack() as st:
            load_x(c, sem, st)
        with nc.Fori(0, DEPTH) as layer:
            c.l = layer
            with phase() as st:
                norm_one(c, st)
            with ExitStack() as st_mix:
                mixer_buffers(c, st_mix)
                with phase() as st:
                    projections(c, st)
                with phase() as st:
                    conv_and_gate(c, st)
                with phase() as st:
                    index_prompt(c, st)
                with phase() as st:
                    attend_prompt(c, st)
                with phase() as st:
                    attend_sample(c, st)
            with ExitStack() as st_ff:
                c.act_lo = sb("act_lo", [P, KC, T], F32R, stack=st_ff)
                with phase() as st:
                    mix_out(c, st)
                with phase() as st:
                    ffn(c, st)
            with phase() as st:
                ffn_norm(c, st)
        with ExitStack() as st:
            store_y(c, sem, st)


def load_x(c, sem, st):
    nc, io = c.nc, c.io
    xt = c.sb("x_tok", [P, 2, D], stack=st)
    xT = c.xT
    const_in, ones_set = sem("const_in"), sem("ones_set")
    x_in = [sem(f"x_in{i}") for i in range(2)]
    turned, copied = sem("x_turned"), sem("x_copied")
    ps = c.ps
    with nc.Block() as block:
        @block.sync
        def _(sp):
            sp.dma_start(c.ident[:, :], io["ident"]).then_inc(const_in, 16)
            sp.dma_start(c.rope_h[:, :, :], io["rope_h"].rearrange("p (n w) -> p n w", n=TILES)).then_inc(const_in, 16)
            sp.dma_start(c.rope_i[:, :, :], io["rope_i"].rearrange("p (n w) -> p n w", n=TILES)).then_inc(const_in, 16)
            sp.dma_start(c.tables[:, :], io["page_table"].rearrange("b p -> (b p)").rearrange("(o n) -> o n", o=1)).then_inc(const_in, 16)
            for n in range(TILES):
                m = tok(n)
                if n >= 2:
                    sp.wait_ge(turned, 2 * (n - 1))
                src = io["x_prompt"][0, n * P:n * P + m, :] if n < PT else io["x_sample"].rearrange("b t d -> (b t) d")
                sp.dma_start(xt[:m, n % 2, :], src).then_inc(x_in[n % 2], 16)

        @block.gpsimd
        def _(pool):
            pool.memset(c.ones[:, :], 1.0).then_inc(ones_set, 1)
            pool.memset(c.eps[:, :], EPS).then_inc(ones_set, 1)

        @block.tensor
        def _(pe):
            pe.wait_ge(const_in, 64)
            for n in range(TILES):
                m = tok(n)
                pe.wait_ge(x_in[n % 2], 16 * (n // 2 + 1))
                for half in range(2):
                    i = 2 * n + half
                    if i >= 4:
                        pe.wait_ge(copied, i - 3)
                    for q in range(4):
                        k = 4 * half + q
                        ins = pe.transpose(ps[:, i % 4, q * P:q * P + m], xt[:m, n % 2, k * P:(k + 1) * P], c.ident[:m, :m])
                    ins.then_inc(turned, 1)

        @block.vector
        def _(dve):
            for n in range(TILES):
                for half in range(2):
                    i = 2 * n + half
                    dve.wait_ge(turned, i + 1)
                    dve.tensor_copy(xT[:, 4 * half:4 * half + 4, cols(n)],
                                    ps[:, i % 4, :].rearrange("p (k t) -> p k t", k=4)[:, :, 0:tok(n)]).then_inc(copied, 1)


def store_y(c, sem, st):
    nc, io = c.nc, c.io
    xT = c.xT
    yt = c.sb("y_tok", [P, 2, D], stack=st)
    turned, copied = sem("y_turned"), sem("y_copied")
    y_out = [sem(f"y_out{i}") for i in range(2)]
    ps = c.ps
    with nc.Block() as block:
        @block.sync
        def _(sp):
            for n in range(TILES):
                m = tok(n)
                sp.wait_ge(copied, 2 * (n + 1))
                dst = io["y_prompt"][0, n * P:n * P + m, :] if n < PT else io["y_sample"].rearrange("b t d -> (b t) d")
                sp.dma_start(dst, yt[:m, n % 2, :]).then_inc(y_out[n % 2], 16)
            sp.wait_ge(y_out[0], 16 * ((TILES + 1) // 2))
            sp.wait_ge(y_out[1], 16 * (TILES // 2))

        @block.tensor
        def _(pe):
            for n in range(TILES):
                m = tok(n)
                for half in range(2):
                    i = 2 * n + half
                    if i >= 4:
                        pe.wait_ge(copied, i - 3)
                    for q in range(4):
                        k = 4 * half + q
                        ins = pe.transpose(ps[:m, i % 4, q * P:(q + 1) * P], xT[:, k, cols(n)], c.ident[:, :])
                    ins.then_inc(turned, 1)

        @block.vector
        def _(dve):
            for n in range(TILES):
                m = tok(n)
                if n >= 2:
                    dve.wait_ge(y_out[n % 2], 16 * (n // 2))
                for half in range(2):
                    i = 2 * n + half
                    dve.wait_ge(turned, i + 1)
                    dve.tensor_copy(yt[:m, n % 2, 512 * half:512 * half + 512], ps[:m, i % 4, :]).then_inc(copied, 1)


def gain(io_g, l):
    return io_g[l].rearrange("(k p) -> p k", p=P)


def norm_one(c, st):
    nc, io, ps, xT = c.nc, c.io, c.ps, c.xT
    sb = lambda n, shape: c.sb(f"a_{n}", shape, stack=st)
    g, sq, acc, rstd = sb("g", [P, KC]), sb("sq", [P, 2, T]), sb("acc", [P, T]), sb("rstd", [P, T])
    s = lambda n: c.layer_sem(f"a_{n}")
    g_in, parked, squared, added, summed, rooted, inverted, h_done = (
        s(n) for n in ("g_in", "parked", "squared", "added", "summed", "rooted", "inverted", "h_done"))
    with nc.Block() as block:
        @block.sync
        def _(sp):
            sp.dma_start(g[:, :], gain(io["g_pre_mix"], c.l)).then_inc(g_in, 16)
            sp.dma_start(c.xpark, xT[:, :, :].rearrange("p k t -> p (k t)")).then_inc(parked, 16)
            sp.wait_ge(parked, 16)

        @block.scalar
        def _(act):
            for k in range(KC):
                if k >= 3:
                    act.wait_ge(added, k - 2)
                act.activation(acc[:, :] if k == 0 else sq[:, k % 2, :], xT[:, k, :], ACT.Square).then_inc(squared, 1)
            act.wait_ge(summed, 1)
            act.activation(by3(rstd[:, :]), ps[:, 0:3, 0:TH], ACT.Sqrt, bias=c.eps[:, 0:1], scale=1.0 / D).then_inc(rooted, 1)

        @block.tensor
        def _(pe):
            pe.wait_ge(added, KC - 1)
            for th in range(3):
                ins = pe.matmul(ps[:, th, 0:TH], c.ones[:, :], acc[:, th * TH:(th + 1) * TH], start=True, stop=True)
            ins.then_inc(summed, 1)

        @block.vector
        def _(dve):
            for k in range(1, KC):
                add_squares(dve, acc, sq, k, squared, added)
            dve.wait_ge(rooted, 1)
            dve.reciprocal(rstd[:, :], rstd[:, :]).then_inc(inverted, 1)
            dve.wait_ge(inverted, 1)
            dve.wait_ge(g_in, 16)
            for k in range(KC):
                dve.scalar_tensor_tensor(out=c.hT[:, k, :], in0=xT[:, k, :], scalar=g[:, k:k + 1], in1=rstd[:, :],
                                         op0=ALU.mult, op1=ALU.mult).then_inc(h_done, 1)


def mixer_buffers(c, st):
    def sb(name, shape, dt=F32):
        return c.sb(name, shape, dt, stack=st)
    c.kT = {"b": c.xT[:, 0:2, :], "c": c.xT[:, 2:4, :]}
    c.qiT = c.xT[:, 4, :]
    c.kiT = c.xT[:, 5, :]
    c.acT = c.xT[:, 6:8, :]
    c.qi_tok = sb("qi_tok", [NS, IXH * IXD])
    c.v = {"b": sb("v_b", [P, TILES, GW]), "c": sb("v_c", [P, TILES, GW])}
    c.chunk = {"b": 2, "c": 4}
    c.wi = sb("wi", [P, TILES, IXH])
    c.mask_c = sb("mask_c", [P, P * PT * (PT + 1) // 2], BF16)
    c.vn = sb("vn", [P, TILES, GW])
    c.ext_p = sb("ext_p", [P, 2, SEQ + 2])
    c.ext_s = sb("ext_s", [P, 2, DB, DT + 2])


def mask_at(n):
    return slice(P * n * (n + 1) // 2, P * (n + 1) * (n + 2) // 2)


def projections(c, st):
    nc, io, ps, hT, l = c.nc, c.io, c.ps, c.hT, c.l
    sb = lambda name, shape: c.sb(name, shape, stack=st)
    W = sb("w_in_slots", [P, 2, KC, 512])
    stage = sb("stage", [P, 2, 512])
    ki4 = sb("ki4", [P, 2, 4, IXD])
    r1, r2 = sb("rope_1", [P, 8, HD // 4]), sb("rope_2", [P, 8, HD // 4])
    st6, mv, ln_r = sb("ln_stats", [P, TILES, 6]), sb("ln_mv", [P, TILES, 2]), sb("ln_r", [P, TILES])
    ln_g, ln_b = sb("ln_g", [P, GW]), sb("ln_b", [P, GW])
    s = c.layer_sem
    w_in = [s(f"w_in{i}") for i in range(2)]
    ln_in = s("ln_in")
    proj_done, proj_freed = s("proj_done"), s("proj_freed")
    rope_1, rope_2, roped = s("rope_1"), s("rope_2"), s("roped")
    tp_done, tp_freed = s("tp_done"), s("tp_freed")
    staged_out = [s(f"staged_out{i}") for i in range(2)]
    v_out = s("v_out")
    mv_set, mv_done, ln_rooted, ln_inv, ln_1, ln_2, ln_done = (s(f"ln_{n}") for n in ("set", "mv", "rooted", "inv", "1", "2", "done"))
    stats_done = s("ln_stats_done")

    groups = [[(C_CV, GW + IXW)], [(C_CQ, 2 * GW)], [(C_BQ, 2 * GW)], [(C_BV, GW), (C_DV, GW)],
              [(C_AH, 2 * GW)], [(C_AC, GW), (C_DU, GW)]]
    TG = 4
    width = [sum(w for _, w in g) for g in groups]
    loads, at = [], [0, 0]
    for g, parts in enumerate(groups):
        at[g % 2] += 16 * len(parts)
        loads.append(at[g % 2])
    items = [(g, n) for g in range(TG) for n in range(TILES)]
    NI = len(items)
    NTP = 3 * TILES
    w_all = io["w_in"][l].rearrange("(k p) n -> p k n", p=P)
    rows = lambda ap, n: ap[0, n * P:(n + 1) * P] if n < PT else None

    def group_load(sp, g):
        o = 0
        for a, w in groups[g]:
            sp.dma_start(W[:, g % 2, :, o:o + w], w_all[:, :, a:a + w]).then_inc(w_in[g % 2], 16)
            o += w

    def kv_rows(name, n):
        if n < PT:
            return io["p_" + name][l][0].rearrange("s h d -> s (h d)")[n * P:(n + 1) * P]
        return io["s_" + name][l].rearrange("b t h d -> (b t) (h d)")

    def kidx_rows(n):
        return io["p_kidx_c"][l][0][n * P:(n + 1) * P] if n < PT else io["s_kidx_c"][l].rearrange("b t d -> (b t) d")

    with nc.Block() as block:
        @block.sync
        def _(sp):
            group_load(sp, 0)
            group_load(sp, 1)
            sp.dma_start(ln_g[:, :], io["ln_g_d"][l].rearrange("(o n) -> o n", o=1).to_broadcast([P, GW])).then_inc(ln_in, 16)
            sp.dma_start(ln_b[:, :], io["ln_b_d"][l].rearrange("(o n) -> o n", o=1).to_broadcast([P, GW])).then_inc(ln_in, 16)
            nv = 0
            for i, (g, n) in enumerate(items):
                m = tok(n)
                if g in (0, 3):
                    sp.wait_ge(proj_freed, i + 1)
                    sp.dma_start(kv_rows("v_c" if g == 0 else "v_b", n), c.v["c" if g == 0 else "b"][:m, n, :]).then_inc(v_out, 16)
                    nv += 1
                if g < 3:
                    sp.wait_ge(roped, i + 1)
                    if g == 0:
                        sp.dma_start(kidx_rows(n), stage[:m, i % 2, 4 * IXD:5 * IXD]).then_inc(staged_out[i % 2], 16)
                    else:
                        sp.dma_start(kv_rows("k_c" if g == 1 else "k_b", n), stage[:m, i % 2, GW:2 * GW]).then_inc(staged_out[i % 2], 16)
                if n == TILES - 1 and g + 2 < len(groups):
                    sp.wait_ge(proj_done, TILES * (g + 1))
                    group_load(sp, g + 2)
            sp.wait_ge(ln_done, TILES)
            sp.dma_start(io["s_v_d"][l].rearrange("b t n -> (b t) n"), c.vn[:NS, PT, :]).then_inc(v_out, 16)
            sp.wait_ge(v_out, 16 * (nv + 1))
            sp.wait_ge(staged_out[0], 16 * ((NTP + 1) // 2))
            sp.wait_ge(staged_out[1], 16 * (NTP // 2))

        @block.tensor
        def _(pe):
            def turn(t):
                g, n = items[t]
                m = tok(n)
                pe.wait_ge(roped, t + 1)
                if t >= 2:
                    pe.wait_ge(tp_freed, t - 1)
                if g == 0:
                    srcs = [stage[:m, t % 2, 0:P], ki4[:m, t % 2, :, :].rearrange("p r d -> p (r d)")]
                else:
                    srcs = [stage[:m, t % 2, q * P:(q + 1) * P] for q in range(4)]
                for q, src in enumerate(srcs):
                    ins = pe.transpose(ps[:, 6 + t % 2, q * P:q * P + m], src, c.ident[:m, :m])
                ins.then_inc(tp_done, 1)

            for i, (g, n) in enumerate(items):
                m = tok(n)
                if n == 0:
                    pe.wait_ge(w_in[g % 2], loads[g])
                if i >= 6:
                    pe.wait_ge(proj_freed, i - 5)
                for k in range(KC):
                    ins = pe.matmul(ps[:m, i % 6, 0:width[g]], hT[:, k, cols(n)], W[:, g % 2, k, 0:width[g]],
                                    start=(k == 0), stop=(k == KC - 1))
                ins.then_inc(proj_done, 1)
                if 1 <= i <= NTP:
                    turn(i - 1)
            for q in range(8):
                g = TG + q // 4
                if q % 4 == 0:
                    pe.wait_ge(w_in[g % 2], loads[g])
                i = NI + 3 * q
                pe.wait_ge(proj_freed, i - 3)
                for k in range(KC):
                    for th in range(3):
                        ins = pe.matmul(ps[:, (i + th) % 6, 0:TH], W[:, g % 2, k, (q % 4) * P:(q % 4 + 1) * P],
                                        hT[:, k, th * TH:(th + 1) * TH], start=(k == 0), stop=(k == KC - 1))
                ins.then_inc(proj_done, 1)

        @block.scalar
        def _(act):
            for i, (g, n) in enumerate(items):
                m = tok(n)
                act.wait_ge(proj_done, i + 1)
                bank = ps[:m, i % 6, :]
                if g in (0, 1, 2) and i >= 2:
                    act.wait_ge(tp_done, i - 1)
                    act.wait_ge(staged_out[i % 2], 16 * ((i - 2) // 2 + 1))
                if g == 0:
                    act.activation(c.v["c"][:m, n, :], bank[:, 0:GW], ACT.Copy)
                    act.activation(stage[:m, i % 2, 0:IXW], bank[:, GW:GW + IXW], ACT.Copy).then_inc(proj_freed, 1)
                elif g < 3:
                    act.activation(stage[:m, i % 2, :], bank[:, 0:2 * GW], ACT.Copy).then_inc(proj_freed, 1)
                else:
                    act.activation(c.v["b"][:m, n, :], bank[:, 0:GW], ACT.Copy)
                    act.activation(c.vn[:m, n, :], bank[:, GW:2 * GW], ACT.Copy).then_inc(proj_freed, 1)
            for q in range(8):
                act.wait_ge(proj_done, NI + q + 1)
                i = NI + 3 * q
                for th in range(3):
                    a, b = th * TH, (th + 1) * TH
                    src = ps[:, (i + th) % 6, :]
                    if q < 2:
                        e = min(b, SEQ)
                        last = act.activation(c.ext_p[:, q, 2 + a:2 + e], src[:, 0:e - a], ACT.Copy)
                        if b > SEQ:
                            last = act.activation(c.ext_s[:, q, :, 2:2 + DT],
                                                  src[:, SEQ - a:TH].rearrange("p (b t) -> p b t", b=DB), ACT.Copy)
                    else:
                        dst = [None, None, c.mT[:, 0], c.mT[:, 1], c.acT[:, 0], c.acT[:, 1], c.mT[:, 6], c.mT[:, 7]][q]
                        last = act.activation(dst[:, a:b], src[:, 0:TH], ACT.Copy)
                    last.then_inc(proj_freed, 1)
            act.wait_ge(mv_done, TILES)
            act.activation(ln_r[:, :], mv[:, :, 1], ACT.Sqrt, bias=c.eps[:, 0:1]).then_inc(ln_rooted, 1)

        @block.vector
        def _(dve):
            def rotate(i):
                g, n = items[i]
                m = tok(n)
                H, w, tab = (5, IXD, c.rope_i) if g == 0 else (8, HD, c.rope_h)
                rot = w // 4
                half = rot // 2
                x = stage[:m, i % 2, 0:H * w].rearrange("p (h w) -> p h w", h=H)
                cs = tab[:m, n, 0:rot].unsqueeze(1).to_broadcast([m, H, rot])
                sn1 = tab[:m, n, rot:rot + half].unsqueeze(1).to_broadcast([m, H, half])
                sn2 = tab[:m, n, rot + half:2 * rot].unsqueeze(1).to_broadcast([m, H, half])
                dve.wait_ge(proj_freed, i + 1)
                if i:
                    dve.wait_ge(roped, i)
                dve.tensor_tensor(r1[:m, 0:H, 0:rot], x[:, :, 0:rot], cs, ALU.mult)
                dve.tensor_tensor(r2[:m, 0:H, 0:half], x[:, :, half:rot], sn1, ALU.mult)
                dve.tensor_tensor(r2[:m, 0:H, half:rot], x[:, :, 0:half], sn2, ALU.mult).then_inc(rope_1, 1)
                dve.wait_ge(rope_1, i + 1)
                last = dve.tensor_tensor(x[:, :, 0:rot], r1[:m, 0:H, 0:rot], r2[:m, 0:H, 0:rot], ALU.add)
                if g == 0:
                    last.then_inc(rope_2, 1)
                    dve.wait_ge(rope_2, i + 1)
                    dve.tensor_copy(ki4[:m, i % 2, :, :], stage[:m, i % 2, 4 * IXD:5 * IXD].unsqueeze(1).to_broadcast([m, 4, IXD]))
                    if n == PT:
                        dve.tensor_copy(c.qi_tok[:, :], stage[:m, i % 2, 0:IXH * IXD])
                    last = dve.tensor_copy(c.wi[:m, n, :], stage[:m, i % 2, 5 * IXD:IXW])
                last.then_inc(roped, 1)

            def unload(t):
                g, n = items[t]
                m = tok(n)
                dve.wait_ge(tp_done, t + 1)
                bank = ps[:, 6 + t % 2, :].rearrange("p (q t) -> p q t", q=4)
                if g == 0:
                    dve.tensor_copy(c.qiT[:, cols(n)], bank[:, 0, 0:m])
                    dve.tensor_copy(c.kiT[:, cols(n)], bank[:, 1, 0:m]).then_inc(tp_freed, 1)
                else:
                    x = "c" if g == 1 else "b"
                    dve.tensor_copy(c.mT[:, c.chunk[x]:c.chunk[x] + 2, cols(n)], bank[:, 0:2, 0:m])
                    dve.tensor_copy(c.kT[x][:, :, cols(n)], bank[:, 2:4, 0:m]).then_inc(tp_freed, 1)

            dve.memset(mv[:, :, :], 1.0).then_inc(mv_set, 1)
            for i in range(NTP):
                rotate(i)
                if i >= 1:
                    unload(i - 1)
            unload(NTP - 1)
            dve.wait_ge(mv_set, 1)
            for n in range(TILES):
                m = tok(n)
                dve.wait_ge(proj_freed, NTP + n + 1)
                dve.bn_stats(st6[:m, n, :], c.vn[:m, n, :]).then_inc(stats_done, 1)
                dve.wait_ge(stats_done, n + 1)
                dve.bn_aggr(mv[:m, n, :], st6[:m, n, :]).then_inc(mv_done, 1)
            dve.wait_ge(ln_rooted, 1)
            dve.reciprocal(ln_r[:, :], ln_r[:, :]).then_inc(ln_inv, 1)
            dve.wait_ge(ln_inv, 1)
            dve.wait_ge(ln_in, 32)
            for n in range(TILES):
                m = tok(n)
                dve.tensor_scalar(c.vn[:m, n, :], c.vn[:m, n, :], mv[:m, n, 0:1], ln_r[:m, n:n + 1],
                                  ALU.subtract, ALU.mult).then_inc(ln_1, 1)
            for n in range(TILES):
                m = tok(n)
                dve.wait_ge(ln_1, n + 1)
                dve.tensor_tensor(c.vn[:m, n, :], c.vn[:m, n, :], ln_g[:m, :], ALU.mult).then_inc(ln_2, 1)
            for n in range(TILES):
                m = tok(n)
                dve.wait_ge(ln_2, n + 1)
                dve.tensor_tensor(c.vn[:m, n, :], c.vn[:m, n, :], ln_b[:m, :], ALU.add).then_inc(ln_done, 1)


def conv_and_gate(c, st):
    nc, io, ps, l = c.nc, c.io, c.ps, c.l
    sb = lambda name, shape: c.sb(name, shape, stack=st)
    cw = sb("conv_w", [P, 2, 3])
    buf = sb("conv_buf", [2 * DB, GW])
    acc_p, acc_s = sb("conv_acc_p", [P, 2, SEQ]), sb("conv_acc_s", [P, 2, DB, DT])
    NST = 2 + 2 * DB
    state, state_t = sb("conv_state", [P, 2, NST]), sb("conv_state_t", [NST, GW])
    ws, wT = sb("w_s", [P, 4, P]), sb("w_sT", [P, 4, P])
    w4 = sb("w_s4", [NS, 4, NS])
    bs = sb("b_s", [P, 2, P])
    gate_p = sb("gate_p", [P, 2, 2, P])
    tril, rep_step, own_step = sb("tril_t", [P, P]), sb("rep_step", [DT, NS]), sb("own_step", [NS, NS])
    s = c.layer_sem
    a_in, d_in = s("conv_in"), s("gate_in")
    buf_turned, buf_set, pad_set, u_done, u2_done = s("buf_turned"), s("buf_set"), s("pad_set"), s("u_done"), s("u2_done")
    tap = s("conv_tap")
    a_done, state_set, state_turned, state_copied, state_out = (s(f"conv_{n}") for n in ("a_done", "state_set", "state_turned", "state_copied", "state_out"))
    ws_turned, ws_masked, w4_made, w4_masked, gated, gate_add, gate_done = (s(f"gate_{n}") for n in ("ws_turned", "ws_masked", "w4_made", "w4_masked", "prod", "add", "done"))

    with nc.Block() as block:
        @block.sync
        def _(sp):
            for k in range(2):
                sp.dma_start(cw[:, k, :], io["conv_w_a"][l].rearrange("i (k p) -> p k i", p=P)[:, k, :]).then_inc(a_in, 16)
            sp.dma_start(buf[:, :], io["cache_conv_a"][l].rearrange("b i n -> (b i) n")).then_inc(a_in, 16)
            sp.dma_start(ws[:, :, :], io["w_s_d"][l].rearrange("g t s -> t g s")).then_inc(d_in, 16)
            sp.dma_start(tril[:, :], io["tril_t"]).then_inc(d_in, 16)
            sp.dma_start(rep_step[:, :], io["rep_step"]).then_inc(d_in, 16)
            sp.dma_start(own_step[:, :], io["own_step"]).then_inc(d_in, 16)
            for g in range(4):
                sp.dma_start(bs[64 * (g % 2):64 * (g % 2) + 64, g // 2, :],
                             io["b_s_d"][l][g:g + 1, :].to_broadcast([64, P])).then_inc(d_in, 16)
            sp.wait_ge(state_copied, 1)
            sp.dma_start(io["p_conv_a"][l].rearrange("b i n -> (b i) n"), state_t[0:2, :]).then_inc(state_out, 16)
            sp.dma_start(io["s_conv_a"][l].rearrange("b i n -> (b i) n"), state_t[2:NST, :]).then_inc(state_out, 16)
            sp.wait_ge(state_out, 32)

        @block.tensor
        def _(pe):
            pe.wait_ge(a_in, 48)
            for k in range(2):
                ins = pe.transpose(ps[:, 0, k * 16:k * 16 + 16], buf[:, k * P:(k + 1) * P], c.ident[:16, :16])
            ins.then_inc(buf_turned, 1)
            pe.wait_ge(d_in, 128)
            for g in range(4):
                ins = pe.transpose(ps[:, 1, g * P:(g + 1) * P], ws[:, g, :], c.ident[:, :])
            ins.then_inc(ws_turned, 1)
            pe.wait_ge(ws_masked, 1)
            pe.matmul(ps[:NS, 2, 0:4 * DT], rep_step[:, :], wT[0:DT, :, 0:DT], start=True, stop=True).then_inc(w4_made, 1)
            for n in range(TILES):
                m = tok(n)
                if n == PT:
                    pe.wait_ge(w4_masked, 4)
                if n >= 2:
                    pe.wait_ge(gate_add, n - 1)
                for g in range(4):
                    rhs = wT[:, g, :] if n < PT else w4[:, g, :]
                    ins = pe.matmul(ps[64 * (g % 2):64 * (g % 2) + 64, 4 + n % 2, (g // 2) * P:(g // 2) * P + m],
                                    c.vn[:m, n, g * 64:(g + 1) * 64], rhs, start=True, stop=True)
                ins.then_inc(gated, 1)
            pe.wait_ge(state_set, 3)
            for k in range(2):
                ins = pe.transpose(ps[:NST, 3, k * P:(k + 1) * P], state[:, k, :], c.ident[:, :])
            ins.then_inc(state_turned, 1)

        @block.vector
        def _(dve):
            dve.memset(c.ext_p[:, :, 0:2], 0.0).then_inc(pad_set, 1)
            dve.wait_ge(buf_turned, 1)
            dve.tensor_copy(c.ext_s[:, :, :, 0:2], ps[:, 0, 0:32].rearrange("p (k b i) -> p k b i", k=2, b=DB)).then_inc(buf_set, 1)
            dve.tensor_tensor(c.ext_p[:, :, 2:], c.ext_p[:, :, 2:], c.acT[:, :, 0:SEQ], ALU.mult).then_inc(u_done, 1)
            for k in range(2):
                dve.tensor_tensor(c.ext_s[:, k, :, 2:], c.ext_s[:, k, :, 2:],
                                  c.acT[:, k, SEQ:].rearrange("p (b t) -> p b t", b=DB), ALU.mult).then_inc(u_done, 1)
            dve.wait_ge(u_done, 3)
            dve.wait_ge(pad_set, 1)
            dve.wait_ge(buf_set, 1)
            dve.tensor_copy(state[:, :, 0:2], c.ext_p[:, :, SEQ:SEQ + 2]).then_inc(state_set, 1)
            for k in range(2):
                dve.tensor_copy(state[:, k, 2:].rearrange("p (b i) -> p b i", b=DB), c.ext_s[:, k, :, DT:DT + 2]).then_inc(state_set, 1)
            nt = 0
            for i in range(3):
                for k in range(2):
                    if i:
                        dve.wait_ge(tap, nt - 3)
                    if i == 0:
                        dve.tensor_scalar(acc_p[:, k, :], c.ext_p[:, k, 0:SEQ], cw[:, k, 0:1], None, ALU.mult).then_inc(tap, 1)
                        dve.tensor_scalar(acc_s[:, k], c.ext_s[:, k, :, 0:DT], cw[:, k, 0:1], None, ALU.mult).then_inc(tap, 1)
                    else:
                        if i:
                            dve.wait_ge(tap, nt - 2)
                        dve.scalar_tensor_tensor(out=acc_p[:, k, :], in0=c.ext_p[:, k, i:i + SEQ], scalar=cw[:, k, i:i + 1],
                                                 in1=acc_p[:, k, :], op0=ALU.mult, op1=ALU.add).then_inc(tap, 1)
                        dve.scalar_tensor_tensor(out=acc_s[:, k], in0=c.ext_s[:, k, :, i:i + DT], scalar=cw[:, k, i:i + 1],
                                                 in1=acc_s[:, k], op0=ALU.mult, op1=ALU.add).then_inc(tap, 1)
                    nt += 2
            dve.wait_ge(tap, 12)
            dve.tensor_tensor(c.mT[:, 0:2, 0:SEQ], c.mT[:, 0:2, 0:SEQ], acc_p[:, :, :], ALU.mult).then_inc(a_done, 1)
            dve.tensor_tensor(c.mT[:, 0:2, SEQ:], c.mT[:, 0:2, SEQ:], acc_s[:, :, :, :].rearrange("p k b t -> p k (b t)"), ALU.mult).then_inc(a_done, 1)
            dve.wait_ge(d_in, 128)
            dve.wait_ge(ws_turned, 1)
            dve.tensor_tensor(wT[:, :, :], ps[:, 1, :].rearrange("p (g t) -> p g t", g=4),
                              tril[:, :].unsqueeze(1).to_broadcast([P, 4, P]), ALU.mult).then_inc(ws_masked, 1)
            dve.wait_ge(w4_made, 1)
            for g in range(4):
                dve.tensor_tensor(w4[:, g, :].rearrange("p (b t) -> p b t", b=DB),
                                  ps[:NS, 2, g * DT:(g + 1) * DT].unsqueeze(1).to_broadcast([NS, DB, DT]),
                                  own_step[:, :].rearrange("p (b t) -> p b t", b=DB), ALU.mult).then_inc(w4_masked, 1)
            for n in range(TILES):
                m = tok(n)
                dve.wait_ge(gated, n + 1)
                for k in range(2):
                    src, dst = ps[:, 4 + n % 2, k * P:k * P + m], gate_p[:, n % 2, k, 0:m]
                    b = bs[:, k, :]
                    if n == PT:
                        src, dst = (x.rearrange("p (b t) -> p b t", b=DB) for x in (src, dst))
                        b = bs[:, k, 0:DT].unsqueeze(1).to_broadcast([P, DB, DT])
                    ins = dve.tensor_tensor(dst, src, b, ALU.add)
                ins.then_inc(gate_add, 1)
                dve.wait_ge(gate_add, n + 1)
                dve.tensor_tensor(c.mT[:, 6:8, cols(n)], c.mT[:, 6:8, cols(n)], gate_p[:, n % 2, :, 0:m], ALU.mult).then_inc(gate_done, 1)
            dve.wait_ge(state_turned, 1)
            dve.tensor_copy(state_t[:, :], ps[:NST, 3, 0:GW]).then_inc(state_copied, 1)


def index_prompt(c, st):
    nc, io, ps = c.nc, c.io, c.ps
    sb = lambda name, shape: c.sb(name, shape, stack=st)
    causal = sb("causal", [P, P])
    relu = sb("index_relu", [P, 2, 4, 512])
    score = sb("index_score", [P, 2, SEQ])
    top = sb("top8", [P, 8])
    s = c.layer_sem
    in_, heads_done, relud, relu_used = s("ix_in"), s("ix_heads"), s("ix_relu"), s("ix_relu_used")
    part, scored, top_found, taken, mask_done = s("ix_part"), s("ix_scored"), s("ix_top"), s("ix_taken"), s("ix_mask")
    items = [(n, a, min(512, (n + 1) * P - a)) for n in range(PT) for a in range(0, (n + 1) * P, 512)]

    with nc.Block() as block:
        @block.sync
        def _(sp):
            sp.dma_start(causal[:, :], io["causal"]).then_inc(in_, 16)

        @block.tensor
        def _(pe):
            for i, (n, a, w) in enumerate(items):
                if i >= 2:
                    pe.wait_ge(relud, i - 1)
                for h in range(IXH):
                    ins = pe.matmul(ps[:, 4 * (i % 2) + h, 0:w], c.qiT[32 * h:32 * h + 32, cols(n)],
                                    c.kiT[32 * h:32 * h + 32, a:a + w], start=True, stop=True)
                ins.then_inc(heads_done, 1)

        @block.scalar
        def _(act):
            for i, (n, a, w) in enumerate(items):
                act.wait_ge(heads_done, i + 1)
                if i >= 2:
                    act.wait_ge(relu_used, i - 1)
                for h in range(IXH):
                    ins = act.activation(relu[:, i % 2, h, 0:w], ps[:, 4 * (i % 2) + h, 0:w], ACT.Relu)
                ins.then_inc(relud, 1)

        @block.vector
        def _(dve):
            np_, nt = 0, 0
            dve.wait_ge(in_, 16)
            for i, (n, a, w) in enumerate(items):
                I = score[:, n % 2, :]
                dve.wait_ge(relud, i + 1)
                dve.tensor_scalar(I[:, a:a + w], relu[:, i % 2, 0, 0:w], c.wi[:, n, 0:1], None, ALU.mult).then_inc(part, 1)
                np_ += 1
                for h in range(1, IXH):
                    dve.wait_ge(part, np_)
                    ins = dve.scalar_tensor_tensor(out=I[:, a:a + w], in0=relu[:, i % 2, h, 0:w], scalar=c.wi[:, n, h:h + 1],
                                                   in1=I[:, a:a + w], op0=ALU.mult, op1=ALU.add)
                    if h < IXH - 1:
                        ins.then_inc(part, 1)
                        np_ += 1
                    else:
                        ins.then_inc(relu_used, 1)
                dve.wait_ge(relu_used, i + 1)
                if a + w < (n + 1) * P:
                    continue
                N = (n + 1) * P
                if n < TOPK // P:
                    m = c.mask_c[:, mask_at(n)]
                    if n:
                        dve.memset(m[:, 0:n * P], 0.0)
                    dve.tensor_copy(m[:, n * P:], causal[:, :]).then_inc(mask_done, 1)
                    continue
                dve.tensor_tensor(I[:, n * P:N], I[:, n * P:N], causal[:, :], ALU.add).then_inc(scored, 1)
                dve.wait_ge(scored, n - TOPK // P + 1)
                for _ in range(TOPK // 8):
                    dve.max(top[:, :], I[:, 0:N]).then_inc(top_found, 1)
                    nt += 1
                    dve.wait_ge(top_found, nt)
                    dve.match_replace(I[:, 0:N], top[:, :], I[:, 0:N], TAKEN).then_inc(taken, 1)
                    dve.wait_ge(taken, nt)
                dve.tensor_scalar(c.mask_c[:, mask_at(n)], I[:, 0:N], TAKEN, NEG, ALU.is_gt, ALU.mult).then_inc(mask_done, 1)


def attend_prompt(c, st):
    nc, io, ps = c.nc, c.io, c.ps
    sb = lambda name, shape, dt=F32: c.sb(name, shape, dt, stack=st)
    bias_b = sb("bias_b", [P, SEQ])
    S = sb("scores", [P, 2, SEQ])
    PTs = sb("probs_t", [P, 2, PT, P])
    O = sb("out_tok", [P, 2, GW])
    mx, sm, rs = sb("row_max", [P, 2]), sb("row_sum", [P, 2]), sb("row_inv", [P, 2])
    s = c.layer_sem
    in_, scored, biased, maxed, exped, turned, unloaded, pv_done, inv_done, out_done, o_turned, o_copied, s_freed = (
        s(f"at_{n}") for n in ("in", "scored", "biased", "maxed", "exped", "turned", "unloaded", "pv", "inv", "out", "o_turned", "o_copied", "s_freed"))
    jobs = [(x, n, h) for x in "bc" for n in range(PT) for h in range(NH)]
    batches = [(j, a, min(4, n + 1 - a)) for j, (x, n, h) in enumerate(jobs) for a in range(0, n + 1, 4)]
    of_job = [[b for b, (jj, _, _) in enumerate(batches) if jj == j] for j in range(len(jobs))]
    J = len(jobs)

    with nc.Block() as block:
        @block.sync
        def _(sp):
            sp.dma_start(bias_b[:, :], io["bias_b"]).then_inc(in_, 16)

        @block.tensor
        def _(pe):
            def score(j):
                x, n, h = jobs[j]
                if j >= 2:
                    pe.wait_ge(biased, j - 1)
                r = 64 * (h % 2)
                N = (n + 1) * P
                for a in range(0, N, 512):
                    w = min(512, N - a)
                    ins = pe.matmul(ps[:, 2 * (j % 2) + a // 512, 0:w], c.mT[r:r + 64, c.chunk[x] + h // 2, cols(n)],
                                    c.kT[x][r:r + 64, h // 2, a:a + w], start=True, stop=True)
                ins.then_inc(scored, 1)

            def turn(j):
                pe.wait_ge(exped, j + 1)
                for b in of_job[j]:
                    _, a, nb = batches[b]
                    if b >= 2:
                        pe.wait_ge(unloaded, b - 1)
                    for q in range(nb):
                        ins = pe.transpose(ps[:, 4 + b % 2, q * P:(q + 1) * P], S[:, j % 2, (a + q) * P:(a + q + 1) * P], c.ident[:, :])
                    ins.then_inc(turned, 1)

            def values(j):
                x, n, h = jobs[j]
                pe.wait_ge(unloaded, of_job[j][-1] + 1)
                if j >= 1:
                    pe.wait_ge(out_done, j)
                for q in range(n + 1):
                    ins = pe.matmul(ps[:, 6, h * HD:(h + 1) * HD], PTs[:, j % 2, q, :], c.v[x][:, q, h * HD:(h + 1) * HD],
                                    start=(q == 0), stop=(q == n))
                ins.then_inc(pv_done, 1)

            def turn_out(t):
                pe.wait_ge(out_done, NH * (t + 1))
                if t >= 1:
                    pe.wait_ge(o_copied, t)
                for k in range(2):
                    ins = pe.transpose(ps[:, 7, k * P:(k + 1) * P], O[:, t % 2, k * P:(k + 1) * P], c.ident[:, :])
                ins.then_inc(o_turned, 1)

            for j in range(J + 2):
                if j < J:
                    score(j)
                if 1 <= j <= J:
                    turn(j - 1)
                if j >= 2:
                    values(j - 2)
                    if (j - 2) % NH == 0 and j - 2 > 0:
                        turn_out((j - 2) // NH - 1)
            turn_out(J // NH - 1)

        @block.scalar
        def _(act):
            def unload(j):
                for b in of_job[j]:
                    _, a, nb = batches[b]
                    act.wait_ge(turned, b + 1)
                    if j >= 2:
                        act.wait_ge(pv_done, j - 1)
                    act.activation(PTs[:, j % 2, a:a + nb, :].rearrange("p b t -> p (b t)"), ps[:, 4 + b % 2, 0:nb * P], ACT.Copy).then_inc(unloaded, 1)

            for j in range(J + 1):
                if j < J:
                    x, n, h = jobs[j]
                    act.wait_ge(maxed, j + 1)
                    if j >= 2:
                        act.wait_ge(inv_done, j - 1)
                    act.activation(S[:, j % 2, 0:(n + 1) * P], S[:, j % 2, 0:(n + 1) * P], ACT.Exp, bias=mx[:, j % 2:j % 2 + 1],
                                   accum_out=sm[:, j % 2:j % 2 + 1]).then_inc(exped, 1)
                if j >= 1:
                    unload(j - 1)

        @block.vector
        def _(dve):
            def norm_out(j):
                x, n, h = jobs[j]
                dve.wait_ge(exped, j + 1)
                dve.reciprocal(rs[:, j % 2:j % 2 + 1], sm[:, j % 2:j % 2 + 1]).then_inc(inv_done, 1)
                dve.wait_ge(inv_done, j + 1)
                dve.wait_ge(pv_done, j + 1)
                if h == 0 and j >= 2 * NH:
                    dve.wait_ge(o_turned, j // NH - 1)
                dve.tensor_scalar(O[:, (j // NH) % 2, h * HD:(h + 1) * HD], ps[:, 6, h * HD:(h + 1) * HD], rs[:, j % 2:j % 2 + 1],
                                  None, ALU.mult).then_inc(out_done, 1)

            def copy_out(t):
                x, n, _ = jobs[t * NH]
                dve.wait_ge(o_turned, t + 1)
                dve.tensor_copy(c.mT[:, c.chunk[x]:c.chunk[x] + 2, cols(n)],
                                ps[:, 7, 0:GW].rearrange("p (k t) -> p k t", k=2)).then_inc(o_copied, 1)

            dve.wait_ge(in_, 16)
            for j in range(J + 2):
                if j < J:
                    x, n, h = jobs[j]
                    N = (n + 1) * P
                    dve.wait_ge(scored, j + 1)
                    if j >= 2:
                        dve.wait_ge(turned, of_job[j - 2][-1] + 1)
                    bias = bias_b[:, SEQ - N:SEQ] if x == "b" else c.mask_c[:, mask_at(n)]
                    dve.scalar_tensor_tensor(out=S[:, j % 2, 0:N], in0=ps[:, 2 * (j % 2):2 * (j % 2) + 2, :].rearrange("p b t -> p (b t)")[:, 0:N],
                                             scalar=SCALE, in1=bias, op0=ALU.mult, op1=ALU.add).then_inc(biased, 1)
                    dve.wait_ge(biased, j + 1)
                    dve.tensor_reduce(mx[:, j % 2:j % 2 + 1], S[:, j % 2, 0:N], AX.X, ALU.max, negate=True).then_inc(maxed, 1)
                if j >= 2:
                    norm_out(j - 2)
                    if (j - 2) % NH == 1 and j - 2 > NH:
                        copy_out((j - 2) // NH - 1)
            copy_out(J // NH - 1)


def attend_sample(c, st):
    nc, io, ps, l = c.nc, c.io, c.ps, c.l
    sb = lambda name, shape, dt=F32: c.sb(name, shape, dt, stack=st)
    flat, used = c.hT[:, :, :].rearrange("p k t -> p (k t)"), [0]

    def of_h(*dims):
        a = used[0]
        used[0] += int(np.prod(dims))
        assert used[0] <= KC * T
        names = "abc"[:len(dims)]
        return flat[:, a:used[0]].rearrange(f"p ({' '.join(names)}) -> p {' '.join(names)}", **dict(zip(names, dims)))

    own = of_h(DB, P)
    rep_heads, sum_heads, new_ok = sb("rep_heads", [NS, P]), sb("sum_heads", [P, NS]), sb("new_ok", [NS, NS])
    bias_sb = sb("bias_sb", [P, BT * P + NS])
    qf = sb("q_rows", [P, 2, P])
    qz = of_h(2, DB, P)
    ixf, ixz = sb("ixq_rows", [P, P]), of_h(DB, P)
    qi4 = sb("ixq_tok", [NS, 4, 4, IXD])
    w_rows, w_cols = sb("wi_rows", [P, 4]), sb("wi_col", [P, 1])
    ki_in = of_h(DB, P)
    ki_t = of_h(DB, P)
    R = sb("ix_relu_s", [P, 512])
    I = sb("ix_score_s", [NS, PAST + NS])
    top = sb("top8_s", [NS, 8])
    kin = sb("k_in", [P, 3, 4, GW])
    kt = c.acT.rearrange("p k t -> p (k t)")[:, 0:2048].rearrange("p (i a t) -> p i a t", i=2, a=2)
    S = of_h(PAST + NS)
    PTs = sb("probs_s_t", [P, PAGES + 1, P])
    VP = 8
    vin = sb("v_in", [P, 2, VP, GW])
    mx, sm, rs = sb("max_s", [P, 1]), sb("sum_s", [P, 1]), sb("inv_s", [P, 1])
    s = c.layer_sem
    names = ("const", "qi4", "ixq_turned", "ixf", "ixz", "w_up", "w_rows", "w_col", "ki_turned", "ki_copied", "ix_heads",
             "ix_relu", "ix_sum", "ix_copied", "ix_mask_add", "top", "taken", "mask", "qf", "qz", "k_turned", "k_copied",
             "qk", "masked", "new_keys", "s_copied", "max", "exp", "inv", "norm", "p_turned", "p_copied", "pv", "out")
    q = {n: s(f"sm_{n}") for n in names}
    ki_sem = s("sm_ki_in")
    ki_used = s("sm_ki_used")
    k_sem = [s(f"sm_k_in{i}") for i in range(3)]
    v_sem = [s(f"sm_v_in{i}") for i in range(2)]
    scol = slice(SEQ, T)
    page_keys = io["cache_kidx_c"][l].rearrange("g (j c) d -> g j (c d)", c=4)
    pool = {"k": io["cache_k_c"][l].rearrange("g s h d -> g s (h d)"), "v": io["cache_v_c"][l].rearrange("g s h d -> g s (h d)")}
    win = {"k": io["cache_k_b"][l].rearrange("b s h d -> b s (h d)"), "v": io["cache_v_b"][l].rearrange("b s h d -> b s (h d)")}
    chunks = {"b": [(0, 4), (4, BT - 4)], "c": [(4 * i, 4) for i in range(CT // 4)]}
    kitems = [(x, ci, a, nt, b) for x in "cb" for ci, (a, nt) in enumerate(chunks[x]) for b in range(DB)]
    vitems = {"c": [(b, a, VP) for b in range(DB) for a in range(0, CT, VP)], "b": [(b, 0, BT) for b in range(DB)]}
    vall = [("c", *v) for v in vitems["c"]] + [("b", *v) for v in vitems["b"]]

    def window_tile(dst, which, b, t):
        if t < FAR_TILES:
            src = win[which][b, t * 16 * (P // DT):(t + 1) * 16 * (P // DT), :].rearrange("(g r) n -> g r n", r=16)[:, 0:DT, :]
            return dst, src
        a = PAST - 512 + (t - FAR_TILES) * P
        return dst, win[which][b, a:a + P, :]

    kat, vat = [], []
    cnt = [0] * 3
    for i, (x, ci, a, nt, b) in enumerate(kitems):
        cnt[i % 3] += 16 * nt
        kat.append(cnt[i % 3])
    cnt = [0] * 2
    for i, (x, b, a, nt) in enumerate(vall):
        cnt[i % 2] += 16 * nt
        vat.append(cnt[i % 2])
    VOFF = len(vitems["c"])
    HC, NC_ = PAST // 512, len(kitems)

    with nc.Block() as block:
        @block.sync
        def _(sp):
            for dst, name in ((own[:, :, :].rearrange("p b t -> p (b t)"), "own_col"), (rep_heads[:, :], "rep_heads"), (sum_heads[:, :], "sum_heads"),
                              (new_ok[:, :], "new_ok"), (bias_sb[:, :], "bias_sb")):
                sp.dma_start(dst, io[name]).then_inc(q["const"], 16)
            for ch in range(HC):
                if ch >= 1:
                    sp.wait_ge(q["ki_turned"], 2 * ch)
                for b in range(DB):
                    for p_ in range(4):
                        i = b * PAGES + 4 * ch + p_
                        page = sp.value_load(c.tables[0:1, i:i + 1], min_val=0, max_val=POOL_PAGES - 1)
                        sp.dma_start(ki_in[32 * p_:32 * p_ + 32, b, :], page_keys[page]).then_inc(ki_sem, 16)

            def load_k(i):
                x, ci, a, nt, b = kitems[i]
                if i >= 3:
                    sp.wait_ge(q["k_turned"], 2 * (i - 2))
                for t in range(nt):
                    dst = kin[:, i % 3, t, :]
                    if x == "c":
                        page = sp.value_load(c.tables[0:1, b * PAGES + a + t:b * PAGES + a + t + 1], min_val=0, max_val=POOL_PAGES - 1)
                        sp.dma_start(dst, pool["k"][page]).then_inc(k_sem[i % 3], 16)
                    else:
                        d_, s_ = window_tile(dst, "k", b, a + t)
                        sp.dma_start(d_, s_).then_inc(k_sem[i % 3], 16)

            def load_v(i):
                x, b, a, nt = vall[i]
                if i >= 2:
                    sp.wait_ge(q["pv"], i - 1)
                for t in range(nt):
                    dst = vin[:, i % 2, t, :]
                    if x == "c":
                        page = sp.value_load(c.tables[0:1, b * PAGES + a + t:b * PAGES + a + t + 1], min_val=0, max_val=POOL_PAGES - 1)
                        sp.dma_start(dst, pool["v"][page]).then_inc(v_sem[i % 2], 16)
                    else:
                        d_, s_ = window_tile(dst, "v", b, a + t)
                        sp.dma_start(d_, s_).then_inc(v_sem[i % 2], 16)

            nkc = sum(1 for k in kitems if k[0] == "c")
            for i in range(nkc):
                load_k(i)
            load_v(0)
            load_v(1)
            for i in range(2, VOFF):
                load_v(i)
            for i in range(nkc, len(kitems)):
                load_k(i)
            for i in range(VOFF, len(vall)):
                load_v(i)

        @block.tensor
        def _(pe):
            pe.wait_ge(q["qi4"], 1)
            for h in range(IXH):
                ins = pe.transpose(ps[:, 0, h * NS:(h + 1) * NS], qi4[:, h, :, :].rearrange("p r d -> p (r d)"), c.ident[:NS, :NS])
            ins.then_inc(q["ixq_turned"], 1)
            pe.wait_ge(q["const"], 80)
            pe.matmul(ps[:, 1, 0:IXH], rep_heads[:, :], c.wi[:NS, PT, :], start=True, stop=True).then_inc(q["w_up"], 1)
            pe.wait_ge(q["ixz"], 1)
            for ch in range(HC):
                pe.wait_ge(ki_sem, 16 * 4 * DB * (ch + 1))
                for half in range(2):
                    i = 2 * ch + half
                    if i >= 1:
                        pe.wait_ge(q["ki_copied"], i)
                    for b in range(4):
                        ins = pe.transpose(ps[:, 2, b * P:(b + 1) * P], ki_in[:, 4 * half + b, :], c.ident[:, :])
                    ins.then_inc(q["ki_turned"], 1)
                pe.wait_ge(q["ki_copied"], 2 * (ch + 1))
                if ch >= 1:
                    pe.wait_ge(q["ix_relu"], ch)
                for r in range(4):
                    for b in range(DB):
                        ins = pe.matmul(ps[:, 4 + r, 0:P], ixz[32 * r:32 * r + 32, b, :], ki_t[32 * r:32 * r + 32, b, :],
                                        start=(b == 0), stop=(b == DB - 1))
                ins.then_inc(q["ix_heads"], 1)
                pe.wait_ge(q["ix_relu"], ch + 1)
                if ch >= 1:
                    pe.wait_ge(q["ix_copied"], ch)
                pe.matmul(ps[:NS, 3, :], sum_heads[:, :], R[:, :], start=True, stop=True).then_inc(q["ix_sum"], 1)
            pe.matmul(ps[:, 4, 0:NS], ixf[0:32, :], c.kiT[0:32, scol], start=True, stop=True).then_inc(q["ix_heads"], 1)
            pe.wait_ge(q["ix_relu"], HC + 1)
            pe.wait_ge(q["ix_copied"], HC)
            pe.matmul(ps[:NS, 3, 0:NS], sum_heads[:, :], R[:, 0:NS], start=True, stop=True).then_inc(q["ix_sum"], 1)

            pe.wait_ge(q["ix_copied"], HC + 1)
            si = 0
            nki = 0
            for xi, x in enumerate("cb"):
                pe.wait_ge(q["qz"], 2 * (xi + 1))
                for ci, (a, nt) in enumerate(chunks[x]):
                    sbank = si % 2
                    if si >= 2:
                        pe.wait_ge(q["s_copied"], si - 1)
                    for b in range(DB):
                        i = nki
                        pe.wait_ge(k_sem[i % 3], kat[i])
                        for hp in range(2):
                            if i >= 1:
                                pe.wait_ge(q["k_copied"], 2 * (i - 1) + hp + 1)
                            for t in range(nt):
                                ins = pe.transpose(ps[:, 2 + hp, t * P:(t + 1) * P], kin[:, i % 3, t, hp * P:(hp + 1) * P], c.ident[:, :])
                            ins.then_inc(q["k_turned"], 1)
                        for hp in range(2):
                            pe.wait_ge(q["k_copied"], 2 * i + hp + 1)
                            ins = pe.matmul(ps[:, sbank, 0:nt * P], qz[:, hp, b, :], kt[:, i % 2, hp, 0:nt * P],
                                            start=(b == 0 and hp == 0), stop=(x == "b" and b == DB - 1 and hp == 1))
                        ins.then_inc(q["qk"], 1)
                        if x == "c" and b == DB - 1:
                            pe.wait_ge(q["mask"], 1)
                            pe.matmul(ps[:, sbank, 0:512], rep_heads[:, :], I[:, ci * 512:(ci + 1) * 512],
                                      start=False, stop=True).then_inc(q["masked"], 1)
                        nki += 1
                    si += 1
                if si >= 2:
                    pe.wait_ge(q["s_copied"], si - 1)
                for hp in range(2):
                    ins = pe.matmul(ps[:, si % 2, 0:NS], qf[:, hp, :], c.kT[x][:, hp, scol], start=(hp == 0), stop=(hp == 1 and x == "b"))
                if x == "c":
                    ins = pe.matmul(ps[:, si % 2, 0:NS], rep_heads[:, :], I[:, PAST:PAST + NS], start=False, stop=True)
                ins.then_inc(q["new_keys"], 1)
                si += 1
                tiles = CT if x == "c" else BT
                pe.wait_ge(q["norm"], xi + 1)
                for bt in range((tiles + 3) // 4 + 1):
                    gi = bt + (0 if x == "c" else CT // 4 + 1)
                    if gi >= 2:
                        pe.wait_ge(q["p_copied"], gi - 1)
                    if bt == (tiles + 3) // 4:
                        ins = pe.transpose(ps[:NS, 4 + gi % 2, 0:P], S[:, tiles * P:tiles * P + NS], c.ident[:, :])
                    else:
                        for t in range(min(4, tiles - 4 * bt)):
                            ins = pe.transpose(ps[:, 4 + gi % 2, t * P:(t + 1) * P], S[:, (4 * bt + t) * P:(4 * bt + t + 1) * P], c.ident[:, :])
                    ins.then_inc(q["p_turned"], 1)
                pe.wait_ge(q["p_copied"], CT // 4 + 1 if x == "c" else CT // 4 + 1 + (BT + 3) // 4 + 1)
                if xi == 1:
                    pe.wait_ge(q["out"], 4)
                for hp in range(2):
                    pe.matmul(ps[:, 6 + hp, 0:64], c.v[x][:NS, PT, hp * P:(hp + 1) * P], PTs[:NS, tiles, hp * 64:(hp + 1) * 64],
                              start=True, stop=False, skip_group_check=True)
                for vi, (b, a, nt) in enumerate(vitems[x]):
                    i = vi + (0 if x == "c" else VOFF)
                    pe.wait_ge(v_sem[i % 2], vat[i])
                    for t in range(nt):
                        for hp in range(2):
                            fin = vi == len(vitems[x]) - 1 and t == nt - 1
                            ins = pe.matmul(ps[:, 6 + hp, 0:64].rearrange("p (h r) -> p h r", h=2)[:, :, b * DT:(b + 1) * DT],
                                            vin[:, i % 2, t, hp * P:(hp + 1) * P],
                                            PTs[:, a + t, hp * 64:(hp + 1) * 64].rearrange("p (h r) -> p h r", h=2)[:, :, b * DT:(b + 1) * DT],
                                            start=False, stop=fin, skip_group_check=True)
                    ins.then_inc(q["pv"], 1)

        @block.scalar
        def _(act):
            def exps(xi):
                N = (CT if xi == 0 else BT) * P + NS
                act.wait_ge(q["max"], xi + 1)
                act.activation(S[:, 0:N], S[:, 0:N], ACT.Exp, bias=mx[:, 0:1], accum_out=sm[:, 0:1]).then_inc(q["exp"], 1)

            for i in range(2 * HC):
                act.wait_ge(q["ki_turned"], i + 1)
                if i >= 2:
                    act.wait_ge(q["ix_heads"], i // 2)
                act.activation(ki_t[:, 4 * (i % 2):4 * (i % 2) + 4, :].rearrange("p b t -> p (b t)"), ps[:, 2, :], ACT.Copy).then_inc(q["ki_copied"], 1)
            for i, (x, ci, a, nt, b) in enumerate(kitems):
                if i >= 2:
                    act.wait_ge(q["qk"], i - 1)
                for hp in range(2):
                    act.wait_ge(q["k_turned"], 2 * i + hp + 1)
                    act.activation(kt[:, i % 2, hp, 0:nt * P], ps[:, 2 + hp, 0:nt * P], ACT.Copy).then_inc(q["k_copied"], 1)
                if i == CT // 4 * DB - 1:
                    exps(0)
            exps(1)

        @block.vector
        def _(dve):
            dve.tensor_copy(qi4[:, :, :, :], c.qi_tok[:, :].rearrange("p (h d) -> p h d", h=IXH).unsqueeze(2).to_broadcast([NS, 4, 4, IXD])).then_inc(q["qi4"], 1)
            dve.wait_ge(q["const"], 80)
            dve.wait_ge(q["ixq_turned"], 1)
            dve.tensor_copy(ixf[:, :], ps[:, 0, 0:P]).then_inc(q["ixf"], 1)
            dve.wait_ge(q["ixf"], 1)
            dve.tensor_tensor(ixz[:, :, :], ixf[:, :].unsqueeze(1).to_broadcast([P, DB, P]), own[:, :, :], ALU.mult).then_inc(q["ixz"], 1)
            dve.wait_ge(q["w_up"], 1)
            for h in range(IXH):
                ins = dve.tensor_copy(w_cols[32 * h:32 * h + 32, :], ps[32 * h:32 * h + 32, 1, h:h + 1])
            ins.then_inc(q["w_col"], 1)
            dve.wait_ge(q["w_col"], 1)
            for ch in range(HC):
                dve.wait_ge(q["ix_heads"], ch + 1)
                if ch >= 1:
                    dve.wait_ge(q["ix_sum"], ch)
                for r in range(4):
                    ins = dve.tensor_scalar(R[:, :].rearrange("p (g j r) -> p g j r", g=4, r=4)[:, :, :, r],
                                            ps[:, 4 + r, 0:P].rearrange("p (g j) -> p g j", g=4), 0.0, w_cols[:, 0:1], ALU.max, ALU.mult)
                ins.then_inc(q["ix_relu"], 1)
                dve.wait_ge(q["ix_sum"], ch + 1)
                dve.tensor_copy(I[:, ch * 512:(ch + 1) * 512], ps[:NS, 3, :]).then_inc(q["ix_copied"], 1)
            dve.wait_ge(q["ix_heads"], HC + 1)
            dve.tensor_scalar(R[:, 0:NS], ps[:, 4, 0:NS], 0.0, w_cols[:, 0:1], ALU.max, ALU.mult).then_inc(q["ix_relu"], 1)
            dve.wait_ge(q["ix_sum"], HC + 1)
            dve.tensor_tensor(I[:, PAST:], ps[:NS, 3, 0:NS], new_ok[:, :], ALU.add).then_inc(q["ix_copied"], 1)
            dve.wait_ge(q["ix_copied"], HC + 1)
            for i in range(TOPK // 8):
                dve.max(top[:, :], I[:, :]).then_inc(q["top"], 1)
                dve.wait_ge(q["top"], i + 1)
                dve.match_replace(I[:, :], top[:, :], I[:, :], TAKEN).then_inc(q["taken"], 1)
                dve.wait_ge(q["taken"], i + 1)
            dve.tensor_scalar(I[:, :], I[:, :], TAKEN, NEG, ALU.is_gt, ALU.mult).then_inc(q["mask"], 1)

            si, gi = 0, 0
            for xi, x in enumerate("cb"):
                if xi:
                    dve.wait_ge(q["new_keys"], 1)
                dve.memset(qf[:, :, :], 0.0).then_inc(q["qf"], 1)
                dve.wait_ge(q["qf"], 3 * xi + 1)
                for hp in range(2):
                    for hl in range(2):
                        h = 2 * hp + hl
                        ins = dve.tensor_copy(qf[64 * hl:64 * hl + 64, hp, h * NS:(h + 1) * NS],
                                              c.mT[64 * hl:64 * hl + 64, c.chunk[x] + hp, scol])
                    ins.then_inc(q["qf"], 1)
                dve.wait_ge(q["qf"], 3 * xi + 3)
                for hp in range(2):
                    dve.tensor_tensor(qz[:, hp, :, :], qf[:, hp, :].unsqueeze(1).to_broadcast([P, DB, P]), own[:, :, :], ALU.mult).then_inc(q["qz"], 1)
                for ci, (a, nt) in enumerate(chunks[x]):
                    if x == "c":
                        dve.wait_ge(q["masked"], ci + 1)
                        dve.tensor_scalar(S[:, a * P:(a + nt) * P], ps[:, si % 2, 0:nt * P], SCALE, None, ALU.mult).then_inc(q["s_copied"], 1)
                    else:
                        if ci == 0:
                            dve.wait_ge(q["p_turned"], CT // 4 + 1)
                        dve.wait_ge(q["qk"], DB * (CT // 4 + ci + 1))
                        dve.scalar_tensor_tensor(out=S[:, a * P:(a + nt) * P], in0=ps[:, si % 2, 0:nt * P], scalar=SCALE,
                                                 in1=bias_sb[:, a * P:(a + nt) * P], op0=ALU.mult, op1=ALU.add).then_inc(q["s_copied"], 1)
                    si += 1
                tiles = CT if x == "c" else BT
                N = tiles * P + NS
                dve.wait_ge(q["new_keys"], xi + 1)
                if x == "c":
                    dve.tensor_scalar(S[:, tiles * P:N], ps[:, si % 2, 0:NS], SCALE, None, ALU.mult).then_inc(q["s_copied"], 1)
                else:
                    dve.scalar_tensor_tensor(out=S[:, tiles * P:N], in0=ps[:, si % 2, 0:NS], scalar=SCALE, in1=bias_sb[:, tiles * P:N],
                                             op0=ALU.mult, op1=ALU.add).then_inc(q["s_copied"], 1)
                si += 1
                dve.wait_ge(q["s_copied"], si)
                dve.tensor_reduce(mx[:, :], S[:, 0:N], AX.X, ALU.max, negate=True).then_inc(q["max"], 1)
                dve.wait_ge(q["exp"], xi + 1)
                dve.reciprocal(rs[:, :], sm[:, :]).then_inc(q["inv"], 1)
                dve.wait_ge(q["inv"], xi + 1)
                dve.tensor_scalar(S[:, 0:N], S[:, 0:N], rs[:, 0:1], None, ALU.mult).then_inc(q["norm"], 1)
                if xi:
                    dve.wait_ge(q["pv"], VOFF)
                nb = (tiles + 3) // 4
                for bt in range(nb + 1):
                    dve.wait_ge(q["p_turned"], gi + 1)
                    if bt == nb:
                        ins = dve.tensor_copy(PTs[:NS, tiles, :], ps[:NS, 4 + gi % 2, 0:P])
                    else:
                        w = min(4, tiles - 4 * bt)
                        ins = dve.tensor_copy(PTs[:, 4 * bt:4 * bt + w, :].rearrange("p b t -> p (b t)"), ps[:, 4 + gi % 2, 0:w * P])
                    ins.then_inc(q["p_copied"], 1)
                    gi += 1
                dve.wait_ge(q["pv"], VOFF if x == "c" else len(vall))
                for hp in range(2):
                    for hl in range(2):
                        dve.tensor_copy(c.mT[64 * hl:64 * hl + 64, c.chunk[x] + hp, scol],
                                        ps[64 * hl:64 * hl + 64, 6 + hp, hl * NS:(hl + 1) * NS]).then_inc(q["out"], 1)


def by3(ap):
    return ap.rearrange("p (a t) -> p a t", a=3)


class WeightStream:

    def __init__(self, c, st, name, blocks, raw, hi, lo):
        self.blocks, self.raw, self.hi, self.lo = blocks, raw, hi, lo
        s = lambda n: c.layer_sem(f"{name}_{n}")
        self.loaded = [s(f"w_loaded{i}") for i in range(2)]
        self.hi_done, self.lo_done, self.used = s("w_hi"), s("w_lo"), s("w_used")

    def load(self, sp, j):
        src = self.blocks[j]
        if j >= 2:
            sp.wait_ge(self.lo_done, j - 1)
        sp.dma_start(self.raw[:, j % 2, 0:src.shape[1], :], src).then_inc(self.loaded[j % 2], 16)

    def split_hi(self, act, j):
        K = self.blocks[j].shape[1]
        act.wait_ge(self.loaded[j % 2], 16 * (j // 2 + 1))
        if j >= 2:
            act.wait_ge(self.used, j - 1)
        act.activation(self.hi[:, j % 2, 0:K, :], self.raw[:, j % 2, 0:K, :], ACT.Copy).then_inc(self.hi_done, 1)

    def split_lo(self, pool, j):
        K = self.blocks[j].shape[1]
        pool.wait_ge(self.hi_done, j + 1)
        pool.tensor_tensor(self.lo[:, j % 2, 0:K, :], self.raw[:, j % 2, 0:K, :], self.hi[:, j % 2, 0:K, :].bitcast(F32),
                           ALU.subtract).then_inc(self.lo_done, 1)

    def multiply(self, pe, j, out, x_hi, x_lo, before_chunk=None):
        K = self.blocks[j].shape[1]
        pe.wait_ge(self.lo_done, j + 1)
        for k in range(K):
            if before_chunk:
                before_chunk(k)
            for i, (w, x) in enumerate(((self.hi, x_hi), (self.hi, x_lo), (self.lo, x_hi))):
                for th in range(3):
                    ins = pe.matmul(out[:, th, :], w[:, j % 2, k, :], x[:, k, th * TH:(th + 1) * TH],
                                    start=(k == 0 and i == 0), stop=(k == K - 1 and i == 2))
        ins.then_inc(self.used, 1)


def mix_out(c, st):
    nc, io, ps, l, xT, mT = c.nc, c.io, c.ps, c.l, c.xT, c.mT
    sb = lambda n, shape, dt=F32: c.sb(f"wo_{n}", shape, dt, stack=st)
    w_all = io["w_o"][l].rearrange("(k p) n -> p k n", p=P)
    W = WeightStream(c, st, "wo", [w_all[:, :, d * P:(d + 1) * P] for d in range(KC)],
                     sb("w_raw", [P, 2, KC, P]), sb("w_hi", [P, 2, KC, P], F32R), sb("w_lo", [P, 2, KC, P], F32R))
    sq, acc, rstd, g = sb("sq", [P, 2, T]), sb("acc", [P, T]), sb("rstd", [P, T]), sb("g", [P, 2, KC])
    s = lambda n: c.layer_sem(f"wo_{n}")
    x_in, g_in, m_hi, m_lo, copied, squared, added, summed, rooted, inverted, scaled, x_done, x_sq, x_add, h_raw, h_hi, h_lo, parked = (
        s(n) for n in ("x_in", "g_in", "m_hi", "m_lo", "copied", "squared", "added", "summed", "rooted", "inverted", "scaled",
                       "x_done", "x_sq", "x_add", "h_raw", "h_hi", "h_lo", "parked"))
    banks = lambda d: ps[:, 3 * (d % 2):3 * (d % 2) + 3, 0:TH]
    with nc.Block() as block:
        @block.sync
        def _(sp):
            W.load(sp, 0)
            W.load(sp, 1)
            sp.dma_start(xT[:, :, :].rearrange("p k t -> p (k t)"), c.xpark).then_inc(x_in, 16)
            sp.dma_start(g[:, 0, :], gain(io["g_post_mix"], l)).then_inc(g_in, 16)
            sp.dma_start(g[:, 1, :], gain(io["g_pre_ffn"], l)).then_inc(g_in, 16)
            for d in range(2, KC):
                W.load(sp, d)
            sp.wait_ge(x_done, KC)
            sp.dma_start(c.xpark, xT[:, :, :].rearrange("p k t -> p (k t)")).then_inc(parked, 16)
            sp.wait_ge(parked, 16)

        @block.tensor
        def _(pe):
            for d in range(KC):
                if d >= 2:
                    pe.wait_ge(copied, d - 1)
                W.multiply(pe, d, banks(d), c.act_hi, c.act_lo, (lambda k: pe.wait_ge(m_lo, k + 1)) if d == 0 else None)
            for r, total in enumerate((added, x_add)):
                pe.wait_ge(total, KC - 1)
                if r == 0:
                    pe.wait_ge(copied, KC)
                else:
                    pe.wait_ge(rooted, 1)
                for th in range(3):
                    ins = pe.matmul(ps[:, th, 0:TH], c.ones[:, :], acc[:, th * TH:(th + 1) * TH], start=True, stop=True)
                ins.then_inc(summed, 1)

        @block.scalar
        def _(act):
            W.split_hi(act, 0)
            for k in range(KC):
                act.activation(c.act_hi[:, k, :], mT[:, k, :], ACT.Copy).then_inc(m_hi, 1)
            for d in range(KC):
                if d + 1 < KC:
                    W.split_hi(act, d + 1)
                act.wait_ge(copied, d + 1)
                if d >= 3:
                    act.wait_ge(added, d - 2)
                act.activation(acc[:, :] if d == 0 else sq[:, d % 2, :], mT[:, d, :], ACT.Square).then_inc(squared, 1)
            for r in range(2):
                act.wait_ge(summed, r + 1)
                act.activation(by3(rstd[:, :]), ps[:, 0:3, 0:TH], ACT.Sqrt, bias=c.eps[:, 0:1], scale=1.0 / D).then_inc(rooted, 1)
                for k in range(KC):
                    if r == 0:
                        act.wait_ge(x_done, k + 1)
                        if k >= 3:
                            act.wait_ge(x_add, k - 2)
                        act.activation(acc[:, :] if k == 0 else sq[:, k % 2, :], xT[:, k, :], ACT.Square).then_inc(x_sq, 1)
                    else:
                        act.wait_ge(h_raw, k + 1)
                        act.activation(c.act_hi[:, k, :], mT[:, k, :], ACT.Copy).then_inc(h_hi, 1)

        @block.gpsimd
        def _(pool):
            for d in range(KC):
                W.split_lo(pool, d)
                if d >= 2:
                    add_squares(pool, acc, sq, d - 1, squared, added)
            add_squares(pool, acc, sq, KC - 1, squared, added)
            for k in range(1, KC):
                add_squares(pool, acc, sq, k, x_sq, x_add)

        @block.vector
        def _(dve):
            for k in range(KC):
                dve.wait_ge(m_hi, k + 1)
                dve.tensor_tensor(c.act_lo[:, k, :], mT[:, k, :], c.act_hi[:, k, :].bitcast(F32), ALU.subtract).then_inc(m_lo, 1)
            for d in range(KC):
                dve.wait_ge(W.used, d + 1)
                if d == 0:
                    dve.wait_ge(m_lo, KC)
                dve.tensor_copy(by3(mT[:, d, :]), banks(d)).then_inc(copied, 1)
            dve.wait_ge(rooted, 1)
            dve.reciprocal(rstd[:, :], rstd[:, :]).then_inc(inverted, 1)
            dve.wait_ge(inverted, 1)
            dve.wait_ge(g_in, 32)
            dve.wait_ge(x_in, 16)
            for k in range(KC):
                dve.scalar_tensor_tensor(out=mT[:, k, :], in0=mT[:, k, :], scalar=g[:, 0, k:k + 1], in1=rstd[:, :],
                                         op0=ALU.mult, op1=ALU.mult).then_inc(scaled, 1)
                dve.wait_ge(scaled, k + 1)
                dve.tensor_tensor(xT[:, k, :], xT[:, k, :], mT[:, k, :], ALU.add).then_inc(x_done, 1)
            dve.wait_ge(rooted, 2)
            dve.reciprocal(rstd[:, :], rstd[:, :]).then_inc(inverted, 1)
            dve.wait_ge(inverted, 2)
            dve.wait_ge(x_done, KC)
            for k in range(KC + 1):
                if k < KC:
                    dve.scalar_tensor_tensor(out=mT[:, k, :], in0=xT[:, k, :], scalar=g[:, 1, k:k + 1], in1=rstd[:, :],
                                             op0=ALU.mult, op1=ALU.mult).then_inc(h_raw, 1)
                if k:
                    dve.wait_ge(h_hi, k)
                    dve.tensor_tensor(c.act_lo[:, k - 1, :], mT[:, k - 1, :], c.act_hi[:, k - 1, :].bitcast(F32), ALU.subtract).then_inc(h_lo, 1)


def add_squares(pool, acc, sq, k, squared, added):
    pool.wait_ge(squared, k + 1)
    if k > 1:
        pool.wait_ge(added, k - 1)
    pool.tensor_tensor(acc[:, :], acc[:, :], sq[:, k % 2, :], ALU.add).then_inc(added, 1)


def ffn(c, st):
    nc, io, ps, l = c.nc, c.io, c.ps, c.l
    fT = c.xT
    PART = KC
    parts = [list(range(a, min(a + PART, FC))) for a in range(0, FC, PART)]
    aT = {n: c.sb(f"a_{n}", [P, PART, T], F32R, stack=st) for n in ("hi", "lo")}
    at = [c.m_at]

    def of_m(name, shape, dt=F32):
        t = nc.alloc_sbuf_tensor_at(name, shape, dt, offset=at[0])
        at[0] += 4 * int(np.prod(shape[1:]))
        assert at[0] <= c.m_at + 4 * KC * T
        return t

    wg, wu, wd = (io[n][l].rearrange("(k p) n -> p k n", p=P) for n in ("w_gate", "w_up", "w_down"))
    blocks, kinds = [], []
    for p_, fs in enumerate(parts):
        for i, f in enumerate(fs):
            blocks += [w[:, :, f * P:(f + 1) * P] for w in (wg, wu)]
            kinds += [("gate", p_, i), ("up", p_, i)]
        for d in range(KC):
            blocks.append(wd[:, fs[0]:fs[-1] + 1, d * P:(d + 1) * P])
            kinds.append(("down", p_, d))
    W = WeightStream(c, st, "ff", blocks, of_m("ff_w_raw", [P, 2, KC, P]), of_m("ff_w_hi", [P, 2, KC, P], F32R), of_m("ff_w_lo", [P, 2, KC, P], F32R))
    sg, a_raw = of_m("ff_silu", [P, T]), of_m("ff_a", [P, T])
    s = lambda n: c.layer_sem(f"ff_{n}")
    freed = [s("freed_even"), s("freed_odd")]
    mul_done, a_hi, a_lo = s("mul"), s("a_hi"), s("a_lo")
    ups = [j for j, kd in enumerate(kinds) if kd[0] == "up"]
    banks = lambda j: ps[:, 3 * (j % 2):3 * (j % 2) + 3, 0:TH]

    with nc.Block() as block:
        @block.sync
        def _(sp):
            for j in range(len(blocks)):
                W.load(sp, j)

        @block.tensor
        def _(pe):
            for j, (kind, p_, i) in enumerate(kinds):
                if j >= 2 and j % 2 == 0:
                    pe.wait_ge(freed[0], j // 2)
                elif j >= 2:
                    prev = kinds[j - 2]
                    if prev[0] == "up":
                        pe.wait_ge(mul_done, sum(len(x) for x in parts[:prev[1]]) + prev[2] + 1)
                    else:
                        pe.wait_ge(freed[1], (KC // 2) * prev[1] + prev[2] // 2 + 1)
                if kind == "down":
                    n = sum(len(x) for x in parts[:p_ + 1])
                    if i == 0:
                        pe.wait_ge(a_lo, n)
                    W.multiply(pe, j, banks(j), aT["hi"], aT["lo"])
                else:
                    W.multiply(pe, j, banks(j), c.act_hi, c.act_lo)

        @block.scalar
        def _(act):
            W.split_hi(act, 0)
            for j, (kind, p_, i) in enumerate(kinds):
                if j + 1 < len(kinds):
                    W.split_hi(act, j + 1)
                if kind == "gate":
                    n = j // 2 - (KC // 2) * p_
                    act.wait_ge(W.used, j + 1)
                    if n:
                        act.wait_ge(mul_done, n)
                    act.activation(by3(sg[:, :]), banks(j), ACT.Silu).then_inc(freed[0], 1)

        @block.gpsimd
        def _(pool):
            for j in range(len(blocks)):
                W.split_lo(pool, j)

        @block.vector
        def _(dve):
            n = 0
            for j, (kind, p_, i) in enumerate(kinds):
                if kind == "gate":
                    continue
                dve.wait_ge(W.used, j + 1)
                if kind == "up":
                    dve.wait_ge(freed[0], j // 2 + 1)
                    if n:
                        dve.wait_ge(a_lo, n)
                    dve.tensor_tensor(by3(a_raw[:, :]), banks(j), by3(sg[:, :]), ALU.mult).then_inc(mul_done, 1)
                    n += 1
                    dve.wait_ge(mul_done, n)
                    dve.tensor_copy(aT["hi"][:, i, :], a_raw[:, :]).then_inc(a_hi, 1)
                    dve.wait_ge(a_hi, n)
                    dve.tensor_tensor(aT["lo"][:, i, :], a_raw[:, :], aT["hi"][:, i, :].bitcast(F32), ALU.subtract).then_inc(a_lo, 1)
                elif p_ == 0:
                    dve.tensor_copy(by3(fT[:, i, :]), banks(j)).then_inc(freed[j % 2], 1)
                else:
                    dve.tensor_tensor(by3(fT[:, i, :]), banks(j), by3(fT[:, i, :]), ALU.add).then_inc(freed[j % 2], 1)


def ffn_norm(c, st):
    nc, io, ps, l, xT = c.nc, c.io, c.ps, c.l, c.xT
    sb = lambda n, shape: c.sb(f"fn_{n}", shape, stack=st)
    xin, sq, acc, rstd, g = sb("x", [P, KC, T]), sb("sq", [P, 2, T]), sb("acc", [P, T]), sb("rstd", [P, T]), sb("g", [P, KC])
    s = lambda n: c.layer_sem(f"fn_{n}")
    x_in, squared, added, summed, rooted, inverted, scaled, x_done = (
        s(n) for n in ("x_in", "squared", "added", "summed", "rooted", "inverted", "scaled", "x_done"))
    with nc.Block() as block:
        @block.sync
        def _(sp):
            sp.dma_start(g[:, :], gain(io["g_post_ffn"], l)).then_inc(x_in, 16)
            sp.dma_start(xin[:, :, :].rearrange("p k t -> p (k t)"), c.xpark).then_inc(x_in, 16)

        @block.tensor
        def _(pe):
            pe.wait_ge(added, KC - 1)
            for th in range(3):
                ins = pe.matmul(ps[:, th, 0:TH], c.ones[:, :], acc[:, th * TH:(th + 1) * TH], start=True, stop=True)
            ins.then_inc(summed, 1)

        @block.scalar
        def _(act):
            for d in range(KC):
                if d >= 3:
                    act.wait_ge(added, d - 2)
                act.activation(acc[:, :] if d == 0 else sq[:, d % 2, :], xT[:, d, :], ACT.Square).then_inc(squared, 1)
            act.wait_ge(summed, 1)
            act.activation(by3(rstd[:, :]), ps[:, 0:3, 0:TH], ACT.Sqrt, bias=c.eps[:, 0:1], scale=1.0 / D).then_inc(rooted, 1)

        @block.vector
        def _(dve):
            for k in range(1, KC):
                add_squares(dve, acc, sq, k, squared, added)
            dve.wait_ge(rooted, 1)
            dve.reciprocal(rstd[:, :], rstd[:, :]).then_inc(inverted, 1)
            dve.wait_ge(inverted, 1)
            dve.wait_ge(x_in, 32)
            for k in range(KC):
                dve.scalar_tensor_tensor(out=xT[:, k, :], in0=xT[:, k, :], scalar=g[:, k:k + 1], in1=rstd[:, :],
                                         op0=ALU.mult, op1=ALU.mult).then_inc(scaled, 1)
                if k:
                    dve.wait_ge(scaled, k)
                    dve.tensor_tensor(xT[:, k - 1, :], xT[:, k - 1, :], xin[:, k - 1, :], ALU.add).then_inc(x_done, 1)
            dve.wait_ge(scaled, KC)
            dve.tensor_tensor(xT[:, KC - 1, :], xT[:, KC - 1, :], xin[:, KC - 1, :], ALU.add).then_inc(x_done, 1)


_INS = ["x_prompt", "x_sample", "cache_conv_a", "cache_k_b", "cache_v_b", "cache_k_c", "cache_v_c", "cache_kidx_c", "page_table",
        "w_in", "conv_w_a", "ln_g_d", "ln_b_d", "w_s_d", "b_s_d", "w_o", "w_gate", "w_up", "w_down",
        "g_pre_mix", "g_post_mix", "g_pre_ffn", "g_post_ffn"]
_OUTS = [("y_prompt", (1, SEQ, D)), ("y_sample", (DB, DT, D)), ("p_conv_a", (DEPTH, 1, 2, GW)),
         ("p_k_b", (DEPTH, 1, SEQ, NH, HD)), ("p_v_b", (DEPTH, 1, SEQ, NH, HD)),
         ("p_k_c", (DEPTH, 1, SEQ, NH, HD)), ("p_v_c", (DEPTH, 1, SEQ, NH, HD)), ("p_kidx_c", (DEPTH, 1, SEQ, IXD)),
         ("s_conv_a", (DEPTH, DB, 2, GW)), ("s_k_b", (DEPTH, DB, DT, NH, HD)), ("s_v_b", (DEPTH, DB, DT, NH, HD)),
         ("s_k_c", (DEPTH, DB, DT, NH, HD)), ("s_v_c", (DEPTH, DB, DT, NH, HD)), ("s_kidx_c", (DEPTH, DB, DT, IXD)),
         ("s_v_d", (DEPTH, DB, DT, GW))]


def build(nc, shapes):
    io = {n: nc.dram_tensor(f"in_{n}", sh, dt, kind="ExternalInput").ap() for n, (sh, dt) in shapes.items()}
    for n, sh in _OUTS:
        io[n] = nc.dram_tensor(f"out_{n}", sh, F32, kind="ExternalOutput").ap()
    program(nc, io)


def kernel(**inputs):
    import concourse.bacc as _bacc
    from concourse.bass_utils import run_bass_kernel_spmd as _run

    nc = _bacc.Bacc("TRN2", target_bir_lowering=False, num_devices=1)
    arrays = {n: np.ascontiguousarray(inputs[n]) for n in _INS}
    arrays.update(CONST)
    build(nc, {n: (a.shape, mybir.dt.from_np(a.dtype)) for n, a in arrays.items()})
    r = _run(nc, [{f"in_{n}": a for n, a in arrays.items()}], core_ids=[0])
    return tuple(r.results[0][f"out_{n}"] for n, _ in _OUTS)
```
